# Optimizing a Trainium2 kernel written in Bass

```python
import math
import jax, jax.numpy as jnp
from jax import lax
import numpy as np

D_MODEL = 1024
BATCH = 1
SEQ = 256
DEPTH = 2
DEC_BATCH = 1
DEC_SEQ = 1024
PAST_LEN = 512

GRID_W = 64
HEAD_DIM = 64
NA_HEADS = 4
NA_KH = 8
NA_KW = 16
DIFF_HEADS = 4
DIFF_QK_DIM = 32
DIFF_V_DIM = 2 * DIFF_QK_DIM
FNET_GROUPS = 4
FNET_GROUP_DIM = 64
SWA_HEADS = 4
SWA_KV_HEADS = 2
SWA_WINDOW = 128
D_FF = 4 * D_MODEL
Q_BLOCK = 128
ROPE_BASE = 10000.0
NORM_EPS = 1e-6
NEG_INF = -1e30

NA_WIDTH = NA_HEADS * HEAD_DIM
DIFF_QK_WIDTH = DIFF_HEADS * 2 * DIFF_QK_DIM
DIFF_WIDTH = DIFF_HEADS * DIFF_V_DIM
FNET_WIDTH = FNET_GROUPS * FNET_GROUP_DIM
SWA_WIDTH = SWA_HEADS * HEAD_DIM
SWA_KV_WIDTH = SWA_KV_HEADS * HEAD_DIM
MIX_WIDTH = NA_WIDTH + DIFF_WIDTH + FNET_WIDTH + SWA_WIDTH
IN_WIDTH = 3 * NA_WIDTH + 2 * DIFF_QK_WIDTH + DIFF_WIDTH + FNET_WIDTH + SWA_WIDTH + 2 * SWA_KV_WIDTH

kernel_name = 'hybrid_diffusion_prefix_trunk_step'

def rmsnorm(x, g):
    xf = x.astype(jnp.float32)
    y = xf * lax.rsqrt(jnp.mean(xf * xf, axis=-1, keepdims=True) + NORM_EPS)
    return (y * g.astype(jnp.float32)).astype(x.dtype)

def modulate(h, shift, scale):
    return h * (1.0 + scale) + shift

def adaln(cond, w, b):
    m = jax.nn.silu(cond) @ w + b
    return jnp.split(m, 6, axis=-1)

def rope_1d(x, pos):
    half = x.shape[-1] // 2
    inv = ROPE_BASE ** (-jnp.arange(half, dtype=jnp.float32) / half)
    ang = pos.astype(jnp.float32)[:, None] * inv[None, :]
    cos = jnp.cos(ang)[:, None, :]
    sin = jnp.sin(ang)[:, None, :]
    xf = x.astype(jnp.float32)
    x1, x2 = xf[..., :half], xf[..., half:]
    return jnp.concatenate([x1 * cos - x2 * sin, x2 * cos + x1 * sin], axis=-1).astype(x.dtype)

def rope_2d(x):
    t = jnp.arange(x.shape[1])
    n = x.shape[-1] // 2
    return jnp.concatenate([rope_1d(x[..., :n], t // GRID_W), rope_1d(x[..., n:], t % GRID_W)], axis=-1)

def split_proj(z):
    B, L = z.shape[:2]
    sizes = (NA_WIDTH, NA_WIDTH, NA_WIDTH, DIFF_QK_WIDTH, DIFF_QK_WIDTH, DIFF_WIDTH,
             FNET_WIDTH, SWA_WIDTH, SWA_KV_WIDTH, SWA_KV_WIDTH)
    cuts = [int(c) for c in np.cumsum(sizes)[:-1]]
    na_q, na_k, na_v, dq, dk, dv, fc, sq, sk, sv = jnp.split(z, cuts, axis=-1)
    return (na_q.reshape(B, L, NA_HEADS, HEAD_DIM), na_k.reshape(B, L, NA_HEADS, HEAD_DIM),
            na_v.reshape(B, L, NA_HEADS, HEAD_DIM),
            dq.reshape(B, L, DIFF_HEADS, 2 * DIFF_QK_DIM), dk.reshape(B, L, DIFF_HEADS, 2 * DIFF_QK_DIM),
            dv.reshape(B, L, DIFF_HEADS, DIFF_V_DIM), fc,
            sq.reshape(B, L, SWA_HEADS, HEAD_DIM), sk.reshape(B, L, SWA_KV_HEADS, HEAD_DIM),
            sv.reshape(B, L, SWA_KV_HEADS, HEAD_DIM))

def dense_attn(q, k, v, sink):
    B, Lq, Hq, d = q.shape
    Hkv = k.shape[2]
    G = Hq // Hkv
    nb = Lq // Q_BLOCK
    scale = d ** -0.5
    qb = q.reshape(B, nb, Q_BLOCK, Hkv, G, d).transpose(1, 0, 2, 3, 4, 5)

    def one(qblk):
        s = jnp.einsum('bqhgd,bkhd->bhgqk', qblk, k).astype(jnp.float32) * scale
        if sink is not None:
            s_sink = jnp.broadcast_to(sink.astype(jnp.float32).reshape(1, Hkv, G, 1, 1), s.shape[:-1] + (1,))
            s = jnp.concatenate([s, s_sink], axis=-1)
        p = jax.nn.softmax(s, axis=-1)
        if sink is not None:
            p = p[..., :-1]
        return jnp.einsum('bhgqk,bkhd->bqhgd', p.astype(v.dtype), v)

    out = lax.map(one, qb)
    return out.transpose(1, 0, 2, 3, 4, 5).reshape(B, Lq, Hq, v.shape[-1])

def diff_lambda(lq1, lk1, lq2, lk2, lambda_init):
    f = jnp.float32
    return (jnp.exp(jnp.sum(lq1.astype(f) * lk1.astype(f)))
            - jnp.exp(jnp.sum(lq2.astype(f) * lk2.astype(f))) + lambda_init)

def diff_attn(q1, q2, k1, k2, v, lam):
    B, L, H, d = q1.shape
    nb = L // Q_BLOCK
    scale = d ** -0.5

    def to_blocks(t):
        return t.reshape(B, nb, Q_BLOCK, H, d).transpose(1, 0, 2, 3, 4)

    def one(qs):
        a, b = qs
        p1 = jax.nn.softmax(jnp.einsum('bqhd,bkhd->bhqk', a, k1).astype(jnp.float32) * scale, axis=-1)
        p2 = jax.nn.softmax(jnp.einsum('bqhd,bkhd->bhqk', b, k2).astype(jnp.float32) * scale, axis=-1)
        p = p1 - lam * p2
        return jnp.einsum('bhqk,bkhe->bqhe', p.astype(v.dtype), v)

    out = lax.map(one, (to_blocks(q1), to_blocks(q2)))
    return out.transpose(1, 0, 2, 3, 4).reshape(B, L, H, v.shape[-1])

def fourier_mix(h, w):
    B, L, _ = h.shape
    hf = h.astype(jnp.float32).reshape(B, L, FNET_GROUPS, FNET_GROUP_DIM)
    y = jnp.fft.fft2(hf, axes=(1, 3), norm='ortho').real.astype(h.dtype)
    return y.reshape(B, L, FNET_WIDTH) @ w

def na_latent(q, k, v, kc, vc, rpb):
    B, N, H, d = q.shape
    rows = N // GRID_W
    kh = min(NA_KH, rows)
    scale = d ** -0.5
    qg = q.reshape(B, rows, GRID_W, H, d)
    kg = k.reshape(B, rows, GRID_W, H, d)
    vg = v.reshape(B, rows, GRID_W, H, d)
    r = jnp.arange(rows)
    rstart = jnp.clip(r - kh // 2, 0, rows - kh)
    ridx = rstart[:, None] + jnp.arange(kh)[None, :]
    kr = kg[:, ridx]
    vr = vg[:, ridx]
    col = jnp.arange(GRID_W)
    cstart = jnp.clip(col - NA_KW // 2, 0, GRID_W - NA_KW)
    cmask = (col[None, :] >= cstart[:, None]) & (col[None, :] < cstart[:, None] + NA_KW)
    dr_i = ridx - r[:, None] + (NA_KH - 1)
    dc_i = jnp.clip(col[None, :] - col[:, None] + (NA_KW - 1), 0, 2 * NA_KW - 2)
    bias = rpb.astype(jnp.float32)[:, dr_i[:, None, :, None], dc_i[None, :, None, :]]
    s_loc = jnp.einsum('brchd,brkwhd->bhrckw', qg, kr).astype(jnp.float32) * scale + bias[None]
    n_loc = kh * GRID_W
    s_loc = jnp.where(cmask[:, None, :], s_loc, NEG_INF).reshape(B, H, rows, GRID_W, n_loc)
    s_ctx = jnp.einsum('brchd,bjhd->bhrcj', qg, kc).astype(jnp.float32) * scale
    p = jax.nn.softmax(jnp.concatenate([s_loc, s_ctx], axis=-1), axis=-1)
    p_loc = p[..., :n_loc].reshape(B, H, rows, GRID_W, kh, GRID_W).astype(v.dtype)
    p_ctx = p[..., n_loc:].astype(v.dtype)
    out = (jnp.einsum('bhrckw,brkwhd->brchd', p_loc, vr)
           + jnp.einsum('bhrcj,bjhd->brchd', p_ctx, vc))
    return out.reshape(B, N, H, d)

def swa_latent(q, k, v, kc, vc, sink):
    B, N, Hq, d = q.shape
    Hkv = k.shape[2]
    G = Hq // Hkv
    W = SWA_WINDOW
    nb = N // W
    Lc = kc.shape[1]
    scale = d ** -0.5
    qb = q.reshape(B, nb, W, Hkv, G, d)
    pad = ((0, 0), (W, W), (0, 0), (0, 0))
    kp = jnp.pad(k, pad)
    vp = jnp.pad(v, pad)
    idx = jnp.arange(nb)[:, None] * W + jnp.arange(3 * W)[None, :]
    kb = kp[:, idx]
    vb = vp[:, idx]
    qpos = jnp.arange(nb)[:, None] * W + jnp.arange(W)[None, :]
    kpos = idx - W
    rel = qpos[:, :, None] - kpos[:, None, :]
    valid = (jnp.abs(rel) <= W) & (kpos[:, None, :] >= 0) & (kpos[:, None, :] < N)
    s_loc = jnp.einsum('bnqhgd,bnkhd->bnhgqk', qb, kb).astype(jnp.float32) * scale
    s_loc = jnp.where(valid[None, :, None, None], s_loc, NEG_INF)
    s_ctx = jnp.einsum('bnqhgd,bjhd->bnhgqj', qb, kc).astype(jnp.float32) * scale
    s_sink = jnp.broadcast_to(sink.astype(jnp.float32).reshape(1, 1, Hkv, G, 1, 1), s_loc.shape[:-1] + (1,))
    p = jax.nn.softmax(jnp.concatenate([s_loc, s_ctx, s_sink], axis=-1), axis=-1)
    p_loc = p[..., :3 * W].astype(v.dtype)
    p_ctx = p[..., 3 * W:3 * W + Lc].astype(v.dtype)
    out = (jnp.einsum('bnhgqk,bnkhd->bnqhgd', p_loc, vb)
           + jnp.einsum('bnhgqj,bjhd->bnqhgd', p_ctx, vc))
    return out.reshape(B, N, Hq, d)

def merge_heads(o_a, o_b, o_c, o_d, w_out):
    B, L = o_c.shape[:2]
    cat = jnp.concatenate([o_a.reshape(B, L, NA_WIDTH), o_b.reshape(B, L, DIFF_WIDTH), o_c,
                           o_d.reshape(B, L, SWA_WIDTH)], axis=-1)
    return cat @ w_out

def mix_context(h, lw):
    na_q, na_k, na_v, dq, dk, dv, fc, sq, sk, sv = split_proj(h @ lw['w_in'])
    o_a = dense_attn(na_q, na_k, na_v, None)
    o_b = diff_attn(dq[..., :DIFF_QK_DIM], dq[..., DIFF_QK_DIM:], dk[..., :DIFF_QK_DIM], dk[..., DIFF_QK_DIM:],
                    dv, lw['lam'])
    o_b = rmsnorm(o_b, lw['subln_g']) * (1.0 - lw['lam_init'])
    o_c = fourier_mix(fc, lw['w_fourier'])
    o_d = dense_attn(sq, sk, sv, lw['sink'])
    return merge_heads(o_a, o_b, o_c, o_d, lw['w_out']), (na_k, na_v, dk, dv, sk, sv)

def mix_latent(h, lw, ck):
    c_na_k, c_na_v, c_diff_k, c_diff_v, c_swa_k, c_swa_v = ck
    na_q, na_k, na_v, dq, dk, dv, fc, sq, sk, sv = split_proj(h @ lw['w_in'])
    o_a = na_latent(na_q, na_k, na_v, c_na_k, c_na_v, lw['rpb'])
    q1 = rope_2d(dq[..., :DIFF_QK_DIM])
    q2 = rope_2d(dq[..., DIFF_QK_DIM:])
    k1 = jnp.concatenate([rope_2d(dk[..., :DIFF_QK_DIM]), c_diff_k[..., :DIFF_QK_DIM]], axis=1)
    k2 = jnp.concatenate([rope_2d(dk[..., DIFF_QK_DIM:]), c_diff_k[..., DIFF_QK_DIM:]], axis=1)
    va = jnp.concatenate([dv, c_diff_v], axis=1)
    o_b = diff_attn(q1, q2, k1, k2, va, lw['lam'])
    o_b = rmsnorm(o_b, lw['subln_g']) * (1.0 - lw['lam_init'])
    o_c = fourier_mix(fc, lw['w_fourier'])
    o_d = swa_latent(rope_2d(sq), rope_2d(sk), sv, c_swa_k, c_swa_v, lw['sink'])
    return merge_heads(o_a, o_b, o_c, o_d, lw['w_out']), ()

def trunk_block(x, mods, g1, g2, w1, w2, mixer):
    sh1, sc1, gt1, sh2, sc2, gt2 = mods
    mixed, ctx_tensors = mixer(modulate(rmsnorm(x, g1), sh1, sc1))
    x = x + gt1 * mixed
    hh = modulate(rmsnorm(x, g2), sh2, sc2)
    x = x + gt2 * (jnp.square(jax.nn.relu(hh @ w1)) @ w2)
    return x, ctx_tensors

def setup_inputs(seed: int = 0) -> dict:
    key = jax.random.key(seed)
    ks = jax.random.split(key, 32)
    D = D_MODEL

    def nrm(k, shape, scale=1.0):
        return jax.random.normal(k, shape, jnp.float32) * scale

    return {
        'x_prompt': nrm(ks[0], (BATCH, SEQ, D)),
        'x_sample': nrm(ks[1], (DEC_BATCH, DEC_SEQ, D)),
        'cache_na_k': nrm(ks[2], (DEC_BATCH, DEPTH, PAST_LEN, NA_HEADS, HEAD_DIM)),
        'cache_na_v': nrm(ks[3], (DEC_BATCH, DEPTH, PAST_LEN, NA_HEADS, HEAD_DIM)),
        'cache_diff_k': nrm(ks[4], (DEC_BATCH, DEPTH, PAST_LEN, DIFF_HEADS, 2 * DIFF_QK_DIM)),
        'cache_diff_v': nrm(ks[5], (DEC_BATCH, DEPTH, PAST_LEN, DIFF_HEADS, DIFF_V_DIM)),
        'cache_swa_k': nrm(ks[6], (DEC_BATCH, DEPTH, PAST_LEN, SWA_KV_HEADS, HEAD_DIM)),
        'cache_swa_v': nrm(ks[7], (DEC_BATCH, DEPTH, PAST_LEN, SWA_KV_HEADS, HEAD_DIM)),
        'c': nrm(ks[8], (DEC_BATCH, D)),
        'c_ctx': nrm(ks[9], (D,)),
        'w_ada': nrm(ks[10], (DEPTH, D, 6 * D), D ** -0.5),
        'b_ada': nrm(ks[11], (DEPTH, 6 * D), 0.02),
        'norm1_g': 1.0 + nrm(ks[12], (DEPTH, D), 0.02),
        'norm2_g': 1.0 + nrm(ks[13], (DEPTH, D), 0.02),
        'w_in': nrm(ks[14], (DEPTH, D, IN_WIDTH), D ** -0.5),
        'na_rpb': nrm(ks[15], (DEPTH, NA_HEADS, 2 * NA_KH - 1, 2 * NA_KW - 1), 0.1),
        'diff_lq1': nrm(ks[16], (DEPTH, DIFF_QK_DIM), 0.1),
        'diff_lk1': nrm(ks[17], (DEPTH, DIFF_QK_DIM), 0.1),
        'diff_lq2': nrm(ks[18], (DEPTH, DIFF_QK_DIM), 0.1),
        'diff_lk2': nrm(ks[19], (DEPTH, DIFF_QK_DIM), 0.1),
        'diff_subln_g': 1.0 + nrm(ks[20], (DEPTH, DIFF_V_DIM), 0.02),
        'w_fourier': nrm(ks[21], (DEPTH, FNET_WIDTH, FNET_WIDTH), FNET_WIDTH ** -0.5),
        'swa_sink': nrm(ks[22], (DEPTH, SWA_HEADS), 0.5),
        'w_out': nrm(ks[23], (DEPTH, MIX_WIDTH, D), MIX_WIDTH ** -0.5),
        'w_mlp1': nrm(ks[24], (DEPTH, D, D_FF), D ** -0.5),
        'w_mlp2': nrm(ks[25], (DEPTH, D_FF, D), D_FF ** -0.5),
        'final_g': 1.0 + nrm(ks[26], (D,), 0.02),
    }

def reference(x_prompt, x_sample, cache_na_k, cache_na_v, cache_diff_k, cache_diff_v, cache_swa_k, cache_swa_v,
              c, c_ctx, w_ada, b_ada, norm1_g, norm2_g, w_in, na_rpb, diff_lq1, diff_lk1, diff_lq2, diff_lk2,
              diff_subln_g, w_fourier, swa_sink, w_out, w_mlp1, w_mlp2, final_g):
    xp = x_prompt
    xs = x_sample
    ctx_out = []
    for l in range(DEPTH):
        lam_init = 0.8 - 0.6 * math.exp(-0.3 * l)
        lw = {
            'w_in': w_in[l], 'rpb': na_rpb[l],
            'lam': diff_lambda(diff_lq1[l], diff_lk1[l], diff_lq2[l], diff_lk2[l], lam_init),
            'lam_init': lam_init, 'subln_g': diff_subln_g[l], 'w_fourier': w_fourier[l],
            'sink': swa_sink[l], 'w_out': w_out[l],
        }
        mods_p = adaln(c_ctx, w_ada[l], b_ada[l])
        xp, kv = trunk_block(xp, mods_p, norm1_g[l], norm2_g[l], w_mlp1[l], w_mlp2[l],
                             lambda h: mix_context(h, lw))
        ctx_out.append(kv)
        mods_s = [m[:, None, :] for m in adaln(c, w_ada[l], b_ada[l])]
        ck = (cache_na_k[:, l], cache_na_v[:, l], cache_diff_k[:, l], cache_diff_v[:, l],
              cache_swa_k[:, l], cache_swa_v[:, l])
        xs, _ = trunk_block(xs, mods_s, norm1_g[l], norm2_g[l], w_mlp1[l], w_mlp2[l],
                            lambda h: mix_latent(h, lw, ck))
    y_prompt = rmsnorm(xp, final_g)
    y_sample = rmsnorm(xs, final_g)
    new_na_k = jnp.stack([t[0] for t in ctx_out], axis=1)
    new_na_v = jnp.stack([t[1] for t in ctx_out], axis=1)
    new_diff_k = jnp.stack([t[2] for t in ctx_out], axis=1)
    new_diff_v = jnp.stack([t[3] for t in ctx_out], axis=1)
    new_swa_k = jnp.stack([t[4] for t in ctx_out], axis=1)
    new_swa_v = jnp.stack([t[5] for t in ctx_out], axis=1)
    return (y_prompt, y_sample, new_na_k, new_na_v, new_diff_k, new_diff_v, new_swa_k, new_swa_v)


_drawn_inputs = setup_inputs


def setup_inputs(seed=0):
    import zlib

    import numpy as np

    out = dict(_drawn_inputs(seed))
    spreads = {}
    factors = {'cache_diff_k': 2.839,
     'cache_swa_k': 2.841,
     'norm1_g': 3.159,
     'norm2_g': 2.743,
     'na_rpb': 8.0,
     'diff_lq1': 3.959,
     'diff_lq2': 7.394,
     'diff_lk2': 5.624,
     'diff_subln_g': 8.0,
     'swa_sink': 64.0,
     'final_g': 7.385,
     'cache_na_k': 8.0,
     'cache_na_v': 8.0}
    for name, (base, spread) in spreads.items():
        noise = np.random.default_rng([zlib.crc32(name.encode()), seed]).standard_normal(out[name].shape)
        drawn = base * np.exp(spread * noise) if base else spread * noise
        out[name] = __import__('jax').numpy.asarray(drawn.astype(out[name].dtype))
    for name, factor in factors.items():
        out[name] = (out[name] * factor).astype(out[name].dtype)
    return out
```

```python
import math
from contextlib import ExitStack

import numpy as np

import concourse.bass as bass
from concourse import mybir

F32 = mybir.dt.float32
F32R = mybir.dt.float32r
ALU = mybir.AluOpType
ACT = mybir.ActivationFunctionType
AX = mybir.AxisListType

P = 128
D = 1024
KT = D // P
SEQ, LAT, PAST, DEPTH = 256, 1024, 512, 2
TOK = LAT + SEQ
KEYS = LAT + PAST + SEQ
GRID_W, NA_KH, NA_KW = 64, 8, 16
ROWS = LAT // GRID_W
HD = 64
W_IN = 2304
D_FF = 4096
EPS = 1e-6
NEG = -1e30
ROPE_BASE = 10000.0
CHUNKS = [(0, 512), (512, 512), (1024, 256)]
NCH = len(CHUNKS)
UW = 256
FS = float(32) ** -0.5
QS = float(HD) ** -0.5

NU_IN, NU_OUT, NB = W_IN // UW, D // UW, D_FF // UW
U_LAYER = NU_IN + NU_OUT + 2 * NB
IN_UNITS = [("t", "A", "q"), ("t", "A", "k"), ("n", "na_v", 0), ("t", "B", "q"), ("t", "B", "k"), ("n", "df_v", 256),
            ("n", "fc", 512), ("t", "D", "q"), ("s", "D", "k")]
CREDIT = 2


def row_window(r):
    return min(max(r - NA_KH // 2, 0), ROWS - NA_KH)


def key_tile0(t):
    return min(max(t - 2, 0), ROWS // 2 - 5)


def constants():
    c = {}
    eye = np.eye(P, dtype=np.float32)
    i = np.arange(P)
    c["ident"] = eye
    c["ones"] = np.ones((P, KEYS), np.float32)
    c["headsum"] = (i[:, None] // HD == i[None, :] // HD).astype(np.float32)
    c["swap"] = np.stack([(i[:, None] == (i[None, :] ^ 8)), (i[:, None] == (i[None, :] ^ 16))]).astype(np.float32)
    ang = 2.0 * np.pi * np.outer(np.arange(HD), np.arange(HD)) / HD
    blk = np.kron(np.eye(2), np.cos(ang)), np.kron(np.eye(2), -np.sin(ang))
    c["dft_ch"] = np.stack(blk).astype(np.float32)
    for name, n in (("lat", LAT), ("ctx", SEQ)):
        a = 2.0 * np.pi * (np.outer(np.arange(n), np.arange(n)) % n) / n
        c["dft_" + name] = np.stack([np.cos(a), np.sin(a)]).astype(np.float32) / np.float32(math.sqrt(n * HD))
    rope = np.zeros((2, 2, P, LAT), np.float32)
    t = np.arange(LAT)
    for kind, d in enumerate((32, HD)):
        n = d // 2
        half = n // 2
        inv = np.float32(ROPE_BASE) ** (-np.arange(half, dtype=np.float32) / np.float32(half))
        for r in range(P):
            j = r % d
            pos = (t // GRID_W) if j < n else (t % GRID_W)
            a = pos.astype(np.float32) * inv[j % half]
            rope[kind, 0, r] = np.cos(a)
            rope[kind, 1, r] = np.sin(a) * (-1.0 if j % n < half else 1.0)
    c["rope"] = rope
    col = np.arange(GRID_W)
    cstart = np.clip(col - NA_KW // 2, 0, GRID_W - NA_KW)
    cmask = (col[None, :] >= cstart[:, None]) & (col[None, :] < cstart[:, None] + NA_KW)

    def allowed(r, rk):
        s = row_window(r)
        return cmask if s <= rk < s + NA_KH else np.zeros_like(cmask)

    m1 = np.zeros((5, P, 640), np.float32)
    for pi, t_ in enumerate((0, 1, 2, 6, 7)):
        for a in range(2):
            for k in range(10):
                ok = allowed(2 * t_ + a, 2 * key_tile0(t_) + k)
                m1[pi, a * 64:a * 64 + 64, k * 64:k * 64 + 64] = np.where(ok, 0.0, NEG)
    c["na_mask_q"] = m1
    mt = np.zeros((2, 6, P, 512), np.float32)
    for ch in range(2):
        for k in range(6):
            for b in range(2):
                for a in range(8):
                    ok = allowed(8 * ch + a, 2 * (2 * ch + k) + b)
                    mt[ch, k, b * 64:b * 64 + 64, a * 64:a * 64 + 64] = np.where(ok.T, 0.0, NEG)
    c["na_mask_k"] = mt
    q, k = i[:, None], i[None, :]
    prev, nxt = np.where(k >= q, 0.0, NEG), np.where(k <= q, 0.0, NEG)
    c["swa_mask_q"] = np.concatenate([prev, np.zeros((P, P)), nxt], 1).astype(np.float32)
    c["swa_mask_k"] = np.concatenate([nxt.T, np.zeros((P, P)), prev.T], 1).astype(np.float32)
    sel = np.zeros((2, P, P), np.float32)
    sel[0, 64, 64:] = 1.0
    sel[1, 64, :64] = 1.0
    c["sink_rows"] = sel
    c["lam_init"] = np.array([0.8 - 0.6 * math.exp(-0.3 * l) for l in range(DEPTH)], np.float32)
    c["pair"] = np.array([[1, 0], [0, 1], [1, 1]], np.float32)
    return c


CONST = constants()


def na_pattern(t):
    return {0: 0, 1: 1, 6: 3, 7: 4}.get(t, 2)


def attention_jobs():
    jobs, v = [], 0
    for kind, heads in (("B", [(h, s) for h in range(4) for s in range(2)]), ("A", [(h, 0) for h in range(4)]),
                        ("D", [(h, 0) for h in range(4)])):
        for h, s in heads:
            for c in range(NCH):
                jobs.append((kind, h, s, c, v))
            v += 1
    return jobs


def row_pieces(kind, c):
    out = []
    if c == 2:
        return [(t, 0, LAT + PAST, SEQ, None) for t in range(2)]
    for t in range(4):
        tt = 4 * c + t
        if kind == "B":
            out += [(t, s, 512 * s, 512, None) for s in range(3)]
        elif kind == "A":
            k0 = key_tile0(tt) * P
            out += [(t, s, k0 + 320 * s, 320, (na_pattern(tt) * 640 + 320 * s)) for s in range(2)]
            out += [(t, 2, LAT, PAST, None)]
        else:
            lo, hi = max(tt - 1, 0), min(tt + 1, LAT // P - 1)
            out += [(t, 0, lo * P, (hi - lo + 1) * P, (lo - tt + 1) * P), (t, 1, LAT, PAST, None)]
    return out


def key_steps(kind, c):
    if c == 2:
        return [(LAT + PAST + P * k, 0, SEQ, None) for k in range(2)]
    out = [(LAT + P * k, 0, 512, None) for k in range(PAST // P)]
    for kt in range(LAT // P):
        if kind == "B":
            out.append((kt * P, 0, 512, None))
            continue
        if kind == "A":
            ts = [t for t in range(4) if key_tile0(4 * c + t) <= kt < key_tile0(4 * c + t) + 5]
        else:
            ts = [t for t in range(4) if abs(4 * c + t - kt) <= 1]
        if ts:
            q0, n = ts[0] * P, len(ts) * P
            tab = (kt - 2 * c) * 512 + q0 if kind == "A" else (4 * c + ts[0] - kt + 1) * P
            out.append((kt * P, q0, n, tab))
    return out


JOBS = attention_jobs()
NJ = len(JOBS)


def n_pieces(j):
    return len(row_pieces(JOBS[j][0], JOBS[j][3]))


def n_steps(j):
    return len(key_steps(JOBS[j][0], JOBS[j][3]))


def attention_slots():
    slots = [("first", 0, list(range(n_pieces(0))))]
    for j in range(NJ):
        s = n_steps(j)
        todo = list(range(n_pieces(j + 1))) if j + 1 < NJ else []
        rate = -(-len(todo) // max(1, s - 3)) if todo else 0
        for i in range(s):
            now, todo = todo[:rate], todo[rate:]
            last = bool(now) and not todo
            slots.append(("step", j, i, now, last))
        assert not todo
        slots.append(("end", j))
    return slots


SLOTS = attention_slots()
PIECES = sum(n_pieces(j) for j in range(NJ))
STEPS = sum(n_steps(j) for j in range(NJ))
PIECE0 = [sum(n_pieces(i) for i in range(j)) for j in range(NJ + 1)]
STEP0 = [sum(n_steps(i) for i in range(j)) for j in range(NJ + 1)]


def in_groups():
    gs = []
    for i, (kind, rows) in enumerate((("A", 0), ("A", 128), ("B", 0), ("B", 128), ("D", 0))):
        gs.append(dict(form="cache", kind=kind, row=rows, unit=-1, col=LAT, n=PAST, dst=("k", kind, rows)))
    for u, (form, kind, what) in enumerate(IN_UNITS):
        if form in "ts":
            for c, (c0, n) in enumerate(CHUNKS):
                for m in range(2 if form == "t" else 1):
                    rope = kind in "BD" and c < 2
                    col = c0 if what == "q" or c < 2 else LAT + PAST
                    gs.append(dict(form="rope" if rope else "t", unit=u, m=m, c=c, n=n, col=col, kind=kind,
                                   scale=QS if (what == "q" and kind != "B") else 1.0, dst=(what, kind, m * P)))
        if form in "ns" or (form == "t" and what == "k"):
            for t in range(TOK // P):
                if form == "t" and t < LAT // P:
                    continue
                gs.append(dict(form="n", unit=u, t=t, n=UW, nform=form))
    return gs


GROUPS = in_groups()
for _u in range(NU_IN):
    [g for g in GROUPS if g["unit"] == _u][-1]["last_of_unit"] = True
    [g for g in GROUPS if g["unit"] == _u][0]["first_of_unit"] = True
    [g for g in GROUPS if g["unit"] == _u][3]["fourth_of_unit"] = True
_t = _r = _n = 0
for _i, _g in enumerate(GROUPS):
    _g["i"] = _i
    if _g["form"] == "n":
        _g["ni"] = _n
        _n += 1
    else:
        _g["ti"] = _t
        _t += 1
    if _g["form"] == "rope":
        _g["ri"] = _r
        _r += 1
NG, NT, NR, NN = len(GROUPS), _t, _r, _n
_h = 0
for _i, _g in enumerate(GROUPS):
    for _x in ([_g] if _g["form"] in ("t", "cache") else []) + ([GROUPS[_i - 1]] if _i and GROUPS[_i - 1]["form"] == "rope" else []):
        _x["hi"] = _h
        _h += 1
assert _h == NT and GROUPS[-1]["form"] != "rope"


def n_stores(g):
    n = 1 if g["nform"] != "t" else 0
    if g["t"] >= LAT // P:
        n += 2 if g["nform"] == "s" else (g["unit"] in (1, 2, 4, 5))
    return n


_b = [0, 0]
for _g in GROUPS:
    if _g["form"] == "n":
        _g["stored_before"] = _b[_g["ni"] % 2]
        _b[_g["ni"] % 2] += 16 * n_stores(_g)
N_BYTES = _b
NDFT = 2 * (LAT // P) + SEQ // P
DFT_USES = [len(range(s, NDFT, 4)) for s in range(4)]
MASKS = (5, 6, 6)
NMASK = 4 * sum(MASKS)
ADDS = [(j, i) for j in range(NJ) for i, s in enumerate(key_steps(JOBS[j][0], JOBS[j][3])) if s[3] is not None]
ADD_INDEX = {ji: n for n, ji in enumerate(ADDS)}
NADD = len(ADDS)
ADD0 = [sum(1 for a in ADDS if a[0] < j) for j in range(NJ + 1)]
HEAD_DMAS = [{"B": 7, "A": 6, "D": 6}[JOBS[v * NCH][0]] + (3 if JOBS[v * NCH][2] == 0 else 0) for v in range(16)]
HEAD_IN = [16 * sum(HEAD_DMAS[u] for u in range(v + 1) if u % 2 == v % 2) for v in range(16)]
HEAD_ALL = [HEAD_IN[14], HEAD_IN[15]]


def is_pair(j):
    return JOBS[j][0] != "B" and JOBS[j][1] % 2 == 1


PAIR_JOBS = [j for j in range(NJ) if is_pair(j)]
NAO = len(PAIR_JOBS) + 2 * NCH
T_USES = [sum(1 for i in range(NT) if i % 2 == b) for b in range(2)]
N_USES = [sum(1 for i in range(NN) if i % 2 == b) for b in range(2)]
R_USES = [sum(1 for i in range(NR) if i % 2 == b) for b in range(2)]
Q_LAYER = NU_OUT * NCH * 2 + NB * NCH * KT
M_LAYER = NB * NCH * 2
NORMS = 2 * DEPTH + 1
FT = KT * NCH
PHASES = 4


def trunk(nc, I, O):
    ctx = ExitStack()

    ctx.enter_context(nc.allow_non_contiguous_dma(reason="small vectors are laid over the partitions"))

    def sem(name):
        return ctx.enter_context(nc.semaphore(name))

    base = -(-nc.sbuf_base // 64) * 64
    top = nc.sbuf_usable_end
    X0 = base
    H0 = X0 + KT * TOK * 4
    W0 = H0 + 2 * KT * TOK * 4
    C0 = W0 + 3 * 16384 + 8192
    cur = {"c": C0}

    def at(name, shape, dt, off):
        size = 4 * int(np.prod(shape[1:]))
        assert off + size <= top, (name, off + size, top)
        return nc.alloc_sbuf_tensor_at(name, shape, dt, offset=off).ap(), off + size

    def put(name, shape, dt=F32):
        ap, cur["c"] = at(name, shape, dt, cur["c"])
        cur["c"] = -(-cur["c"] // 32) * 32
        return ap

    xT, _ = at("xT", [P, KT, TOK], F32, X0)
    h_hi, _ = at("h_hi", [P, KT, TOK], F32R, H0)
    h_lo, _ = at("h_lo", [P, KT, TOK], F32R, H0 + KT * TOK * 4)
    w_hi, w_lo = [], []
    for s in range(3):
        a, o = at(f"w_hi{s}", [P, 2048], F32R, W0 + s * 16384)
        b, _ = at(f"w_lo{s}", [P, 2048], F32R, o)
        w_hi.append(a)
        w_lo.append(b)
    stage, _ = at("stage", [P, 2048], F32, W0 + 3 * 16384)
    ident = put("ident", [P, P])
    ones = put("ones_sq", [P, P])
    headsum = put("headsum", [P, P])
    swap = put("swap", [P, 2, P])
    pair = put("pair", [3, 2])
    mods = put("mods", [P, 48, 2])
    gains = put("gains", [P, 3, KT])
    mod_a = put("mod_a", [P, 2, KT, 2])
    fin_a = put("fin_a", [P, KT, 2])
    zero8 = put("zero8", [P, 8])
    eps_c = put("eps_c", [P, 1])
    cond = put("cond", [P, KT, 2])
    cond_t = put("cond_t", [P, 3, KT, 2])
    lam_v = put("lam_v", [P, 4, 32])
    lam_s = put("lam_s", [P, 8])
    lam_i = put("lam_i", [P, 1])
    sub_g = put("sub_g", [P, 2])
    sink_c = put("sink_c", [P, 4])
    TMP = cur["c"]

    def tmp(start=None):
        cur["c"] = TMP if start is None else start

    tmp()
    sq = [put(f"sq{i}", [P, 512]) for i in range(2)]
    xr = [put(f"xr{i}", [P, 512]) for i in range(2)]
    hf = [put(f"hf{i}", [P, 512]) for i in range(2)]
    std = put("std", [P, 512])
    rstd = [put(f"rstd{i}", [P, 512]) for i in range(2)]
    TMP2 = cur["c"]
    zf = [put(f"zf{i}", [P, 512]) for i in range(2)]
    z_hi = [put(f"z_hi{i}", [P, 512], F32R) for i in range(2)]
    z_lo = [put(f"z_lo{i}", [P, 512], F32R) for i in range(2)]
    vn = [put(f"vn{i}", [P, UW]) for i in range(2)]
    cache_n = put("cache_n", [P, 4, P])
    tmp()
    rope_t = [put(f"rope_t{i}", [P, 2, 512]) for i in range(2)]
    rp1 = put("rp1", [P, 512])
    rp2 = [put(f"rp2{i}", [P, 512]) for i in range(2)]
    zr = [put("zr0", [P, 512])]
    assert cur["c"] <= TMP2
    tmp(TMP2)
    m_hi = [put(f"m_hi{i}", [P, 2, 512], F32R) for i in range(2)]
    m_lo = [put(f"m_lo{i}", [P, 2, 512], F32R) for i in range(2)]
    m_r = [put(f"m_r{i}", [P, 512]) for i in range(2)]
    m_f = [put(f"m_f{i}", [P, 512]) for i in range(2)]
    ada_w = []
    off = H0
    for s in range(4):
        a, off = at(f"ada_w{s}", [P, KT, 512], F32, off)
        ada_w.append(a)
    m_row, _ = at("m_row", [3, 4, 512], F32, off)
    x_nat, _ = at("x_nat", [P, TOK // P, D], F32, W0)
    off = H0
    fc_n, off = at("fc_n", [P, TOK // P, 256], F32, off)
    dft_t = []
    for s in range(4):
        a, off = at(f"dft_t{s}", [P, 2, 512], F32, off)
        dft_t.append(a)
    f_ab, off = at("f_ab", [P, 4, 512], F32, off)
    w_f, off = at("w_f", [P, 2, 256], F32, off)
    dft_ch, off = at("dft_ch", [P, 2, P], F32, off)
    g_cs, off = at("g_cs", [P, 2, 2, 256], F32, off)
    off = H0
    q1, q2, k1, k2, vv = [], [], [], [], []
    for s in range(2):
        for lst, nm, shp, dt in ((q1, "q1", [P, TOK], F32R), (q2, "q2", [96, TOK], F32R), (k1, "k1", [P, KEYS], F32R),
                                 (k2, "k2", [96, KEYS], F32R), (vv, "vv", [P, KEYS // P, P], F32)):
            a, off = at(f"{nm}_{s}", shp, dt, off)
            lst.append(a)
    NP_RING = 8
    prob = []
    for s in range(NP_RING):
        a, off = at(f"prob{s}", [P, 512], F32, off)
        prob.append(a)
    assert off <= W0
    off = W0
    na_q, off = at("na_q", [P, 5 * 640], F32, off)
    na_k = []
    for c in range(2):
        a, off = at(f"na_k{c}", [P, 6 * 512], F32, off)
        na_k.append(a)
    o_b, off = at("o_b", [P, 2, TOK], F32, off)
    o_ad, off = at("o_ad", [P, TOK], F32, off)
    assert off <= C0
    cur["c"] = TMP
    swa_q, swa_k = put("swa_q", [P, 384]), put("swa_k", [P, 384])
    sink_rows = put("sink_rows", [P, 2, P])
    na_m = [put(f"na_m{i}", [P, 640]) for i in range(2)]
    mp = put("mp", [P, 4, 4])
    mcol = [put(f"mcol{i}", [P, 4]) for i in range(2)]
    junk = put("junk", [P, 2, 384])
    sb = [put(f"sb{i}", [P, 512]) for i in range(2)]
    rden = put("rden", [P, 512])
    o_t = put("o_t", [P, 512])
    p_sink = put("p_sink", [P, 512])
    ao_hi = [put(f"ao_hi{i}", [P, 512], F32R) for i in range(2)]
    ao_lo = [put(f"ao_lo{i}", [P, 512], F32R) for i in range(2)]
    y_nat, _ = at("y_nat", [P, TOK // P, D], F32, W0)
    pad_zero, _ = at("pad_zero", [4, 23 * 127], F32, W0 + 40960)

    bank = ctx.enter_context(nc.psum_tensor("bank", [P, 8, 512], F32))

    def scratch(name, shape):
        return nc.dram_tensor(name, shape, F32).ap()

    s_q = {k: scratch(f"s_q{k}", [2, 256, TOK]) for k in "ABD"}
    s_k = {k: scratch(f"s_k{k}", [2, 256 if k != "D" else P, KEYS]) for k in "ABD"}
    s_v = scratch("s_v", [TOK, 1024])
    s_o = scratch("s_o", [2, D, TOK])
    s_mods = scratch("s_mods", [DEPTH, P, 96])
    PADR, PADC = 23, 127
    s_pad = scratch("s_pad", [DEPTH, 4, 2, PADR, PADC])

    s_ones = scratch("s_ones", [1, KEYS])
    s_toe = scratch("s_toe", [DEPTH, 4, 2, 64, PADR * 64])

    toe_in = sem("toe_in")
    phase = sem("phase")
    ada_ok, seen = sem("ada_ok"), sem("seen")
    const_in = sem("const_in")
    misc = sem("misc")
    xin = sem("xin")
    cond_rdy, cond_e, cond_d = sem("cond_rdy"), sem("cond_e"), sem("cond_d")
    ada_in = [sem(f"ada_in{i}") for i in range(4)]
    ada_rows, ada_copied, ada_used, ada_modp, ada_mods, ada_saved = (sem("ada_rows"), sem("ada_copied"), sem("ada_used"),
                                                          sem("ada_modp"), sem("ada_mods"), sem("ada_saved"))
    xt_full, xt_free = sem("xt_full"), sem("xt_free")
    small_in, small_rdy, mod_rdy = sem("small_in"), sem("small_rdy"), sem("mod_rdy")
    stage_full, whi_rdy, wlo_rdy, w_used = sem("stage_full"), sem("whi_rdy"), sem("wlo_rdy"), sem("w_used")
    n_sq, n_squ, n_std, n_rs, n_t, n_f, n_hi, n_lo = (sem("n_sq"), sem("n_squ"), sem("n_std"), sem("n_rs"), sem("n_t"),
                                                      sem("n_f"), sem("n_hi"), sem("n_lo"))
    z_full = sem("z_full")
    zf_rdy, rp_full, rp_1, rp_2, zr_rdy, zhi_rdy, zlo_rdy = (sem("zf_rdy"), sem("rp_full"), sem("rp_1"), sem("rp_2"),
                                                             sem("zr_rdy"), sem("zhi_rdy"), sem("zlo_rdy"))
    z_out = [sem(f"z_out{i}") for i in range(2)]
    vn_rdy = sem("vn_rdy")
    vn_out = [sem(f"vn_out{i}") for i in range(2)]
    rope_in = [sem(f"rope_in{i}") for i in range(2)]
    cache_in = sem("cache_in")
    f_in = sem("f_in")
    dft_in = [sem(f"dft_in{i}") for i in range(4)]
    dft_used, f_gp, f_g, f_full, f_ev, f_o, f_hi, f_lo = (sem("dft_used"), sem("f_gp"), sem("f_g"), sem("f_full"), sem("f_ev"),
                                                    sem("f_o"), sem("f_hi"), sem("f_lo"))
    f_out = [sem(f"f_out{i}") for i in range(2)]
    a_init, a_tab = sem("a_init"), sem("a_tab")
    head_in = [sem(f"head_in{i}") for i in range(2)]
    b_in = [sem(f"b_in{i}") for i in range(3)]
    b_rdy = sem("b_rdy")
    nm_in = [sem(f"nm_in{i}") for i in range(2)]
    s1_full, s1_max, m_col, m_rowp, m_rdy = sem("s1_full"), sem("s1_max"), sem("m_col"), sem("m_rowp"), sem("m_rdy")
    s2_full, s2_add, p_rdy, pv_done = sem("s2_full"), sem("s2_add"), sem("p_rdy"), sem("pv_done")
    sink_p, o_full, o_den, o_mul, o_free = sem("sink_p"), sem("o_full"), sem("o_den"), sem("o_mul"), sem("o_free")
    ao_h, ao_l = sem("ao_h"), sem("ao_l")
    ao_out = [sem(f"ao_out{i}") for i in range(2)]
    sn_sq, sn_full, sn_std, sn_r, sn_o = sem("sn_sq"), sem("sn_full"), sem("sn_std"), sem("sn_r"), sem("sn_o")
    lam_d, lam_e = sem("lam_d"), sem("lam_e")
    o_in = [sem(f"o_in{i}") for i in range(NCH)]
    q_full, q_free = sem("q_full"), sem("q_free")
    p1_full, r_rdy, sqr_rdy, mhi_rdy, mlo_rdy = (sem("p1_full"), sem("r_rdy"), sem("sqr_rdy"), sem("mhi_rdy"),
                                                 sem("mlo_rdy"))
    y_full, y_ev, y_out = sem("y_full"), sem("y_ev"), sem("y_out")

    def settle(e):
        e.sem_inc(seen, 1)

    def barrier(e, k):
        settle(e)
        e.drain().then_inc(phase, 1)
        e.wait_ge(phase, 5 * k)
        settle(e)

    SLOT_OUT = [0, 2, 1, 2]

    def unit_slot(n):
        if n < NU_IN:
            return n % 3
        if n < NU_IN + NU_OUT:
            return SLOT_OUT[n - NU_IN]
        b, down = divmod(n - NU_IN - NU_OUT, 2)
        return 2 if down else b % 2

    def unit_prev(n):
        if n < NU_IN:
            return n - 3 if n >= 3 else None
        if n < NU_IN + NU_OUT:
            return NU_IN + 1 if n == NU_IN + 3 else None
        return n - 2 if (n - NU_IN - NU_OUT) % 2 else n - 4

    def hi_unit(pool, l, n, slot, prev):
        pool.wait_ge(stage_full, (l * U_LAYER + n + 1) * 16)
        if prev is not None:
            pool.wait_ge(w_used, l * U_LAYER + prev + 1 + 1)
        settle(pool)
        pool.tensor_scalar(w_hi[slot], stage, 1.0, 0.0, ALU.mult, ALU.add).then_inc(whi_rdy, 1)

    def lo_unit(dve, l, n, slot):
        dve.wait_ge(whi_rdy, l * U_LAYER + n + 1)
        dve.tensor_tensor(w_lo[slot], stage, w_hi[slot].bitcast(F32), ALU.subtract).then_inc(wlo_rdy, 1)

    def load_unit(sp, l, n, src):
        sp.wait_ge(wlo_rdy, l * U_LAYER + n + 1)
        sp.dma_start(stage.rearrange("p (k n) -> p k n", k=src.shape[1]), src).then_inc(stage_full, 16)

    w_in_v = I["w_in"].rearrange("l (k p) n -> l p k n", p=P)
    w_out_v = I["w_out"].rearrange("l (k p) n -> l p k n", p=P)
    w1_v = I["w_mlp1"].rearrange("l (k p) n -> l p k n", p=P)
    w2_v = I["w_mlp2"].rearrange("l (k p) n -> l p k n", p=P)
    w_ada_v = I["w_ada"].rearrange("l (k p) n -> l p k n", p=P)

    def norm_act(act, nn, x_at, final=None):
        def squares(c):
            c0, n = CHUNKS[c]
            x_at(act, c)
            for k in range(KT):
                i = (nn * NCH + c) * KT + k
                act.wait_ge(n_squ, i + 1)
                act.activation(sq[k % 2][:, :n], xT[:, k, c0:c0 + n], ACT.Square).then_inc(n_sq, 1)
            act.wait_ge(n_squ, (nn * NCH + c + 1) * KT + CREDIT)
            act.wait_ge(n_rs, nn * NCH + c + 1 + 1)
            act.activation(std[:, :n], bank[:, 6 + c % 2, :n], ACT.Sqrt, bias=eps_c, scale=1.0 / D).then_inc(n_std, 1)

        def upper(c):
            c0, n = CHUNKS[c]
            for k in range(KT):
                i = (nn * NCH + c) * KT + k
                act.wait_ge(n_f, i + 1 + CREDIT)
                act.activation(h_hi[:, k, c0:c0 + n], hf[k % 2][:, :n], ACT.Copy).then_inc(n_hi, 1)

        squares(0)
        for c in range(NCH):
            if c + 1 < NCH:
                squares(c + 1)
            if final:
                final(c)
            else:
                upper(c)

    def norm_pe(pe, nn, c):
        n = CHUNKS[c][1]
        for k in range(KT):
            i = (nn * NCH + c) * KT + k
            if k == 0:
                pe.wait_ge(n_std, nn * NCH + c + 1)
            pe.wait_ge(n_sq, i + 1)
            pe.matmul(bank[:, 6 + c % 2, :n], ones, sq[k % 2][:, :n], start=(k == 0),
                      stop=(k == KT - 1)).then_inc(n_squ, 1)

    def norm_dve(dve, nn, final=False):
        for c in range(NCH):
            c0, n = CHUNKS[c]
            q = nn * NCH + c
            dve.wait_ge(n_std, q + 1 + CREDIT)
            if c >= 2:
                dve.wait_ge(n_t, (q - 1) * KT)
            dve.reciprocal(rstd[c % 2][:, :n], std[:, :n]).then_inc(n_rs, 1)
            dve.wait_ge(n_rs, q + 1 + CREDIT)

            def lower(k):
                dve.wait_ge(n_hi, q * KT + k + 1 + CREDIT)
                dve.tensor_tensor(h_lo[:, k, c0:c0 + n], hf[k % 2][:, :n], h_hi[:, k, c0:c0 + n].bitcast(F32),
                                  ALU.subtract).then_inc(n_lo, 1)
            for k in range(KT):
                i = q * KT + k
                dve.wait_ge(n_f, i + 1)
                dve.tensor_tensor(xr[k % 2][:, :n], xT[:, k, c0:c0 + n], rstd[c % 2][:, :n], ALU.mult).then_inc(n_t, 1)
                if k and not final:
                    lower(k - 1)
            if not final:
                lower(KT - 1)

    def norm_pool(pool, nn, scale, shift, final=False):
        for c in range(NCH):
            n = CHUNKS[c][1]
            cd = 1 if c == 2 else 0
            for k in range(KT):
                i = (nn * NCH + c) * KT + k
                pool.wait_ge(n_t, i + 1)
                if final:
                    pool.wait_ge(y_full, (c * KT + k) + 1)
                else:
                    pool.wait_ge(n_hi, i + 1)
                    pool.wait_ge(n_lo, i + 1)
                settle(pool)
                pool.tensor_scalar(hf[k % 2][:, :n], xr[k % 2][:, :n], scale(k, cd), shift(k, cd), ALU.mult,
                                   ALU.add).then_inc(n_f, 1)

    def ones_row(n):
        return s_ones[0:1, 0:n]

    def fourier_store(sp, l, c):
        c0, n = CHUNKS[c]
        for m in range(2):
            sp.wait_ge(f_lo, (l * NCH + c) * 2 + m + 1)
            for part, src in ((0, ao_hi[m]), (1, ao_lo[m])):
                sp.dma_start(s_o[part, 512 + m * P:512 + (m + 1) * P, c0:c0 + n], src[:, :n].bitcast(F32)
                             ).then_inc(f_out[m], 16)

    def y_ev_at(t):
        return (min(t // 4, 2) + 1) * KT

    block = ctx.enter_context(nc.Block())

    @block.sync
    def _(sp):
        sp.sem_inc(ada_ok, 1)
        for dst, src in ((ident, I["k_ident"]), (ones, I["k_ones"][:, 0:P]), (headsum, I["k_headsum"]),
                         (swap, I["k_swap"].rearrange("s p n -> p s n")), (pair, I["k_pair"]),
                         (fin_a[:, :, 0], I["final_g"].rearrange("(k p) -> p k", p=P))):
            sp.dma_start(dst, src).then_inc(const_in, 16)
        sp.dma_start(cond[:, :, 0], I["c"].rearrange("b (k p) -> p (b k)", p=P)).then_inc(const_in, 16)
        sp.dma_start(cond[:, :, 1], I["c_ctx"].rearrange("(k p) -> p k", p=P)).then_inc(const_in, 16)
        for t in range(TOK // P):
            src = I["x_sample"][0, t * P:(t + 1) * P] if t < LAT // P else I["x_prompt"][0, t * P - LAT:(t + 1) * P - LAT]
            sp.dma_start(x_nat[:, t], src).then_inc(xin, 16)
        with sp.Fori(0, DEPTH) as l:
            for n in range(12):
                s = n % 4
                sp.wait_ge(ada_used, l * 12 + n + 1)
                sp.dma_start(ada_w[s], w_ada_v[l, :, :, n * 512:(n + 1) * 512]).then_inc(ada_in[s], 16)
                sp.dma_start(m_row[2:3, s], I["b_ada"][l, n * 512:(n + 1) * 512].rearrange("(a n) -> a n", a=1)
                             ).then_inc(ada_in[s], 16)
            sp.wait_ge(ada_mods, l + 1 + 1)
            sp.dma_start(s_mods[l], mods.rearrange("p a b -> p (a b)")).then_inc(ada_saved, 16)
            sp.wait_ge(ada_saved, l * 16 + 16)
            sp.sem_inc(ada_ok, 1)
        sp.wait_ge(misc, 1)
        for l in range(DEPTH):
            for r in range(2):
                sp.dma_start(s_pad[l, :, r].rearrange("h a b -> h (a b)"), pad_zero).then_inc(small_in, 16)
        sp.wait_ge(small_in, 4 * 16)
        for l in range(DEPTH):
            for r in range(2):
                for h in range(4):
                    sp.dma_start(s_pad[l, h, r, 4:19, 48:79], (I["na_rpb"] if r == 0 else I["na_rpb_rev"])[l, h]
                                 ).then_inc(small_in, 16)
        sp.wait_ge(small_in, (4 + 16) * 16)
        for l in range(DEPTH):
            for h in range(4):
                for r in range(2):
                    off = ((l * 4 + h) * 2 + r) * PADR * PADC + 63
                    src = bass.AP(tensor=s_pad.tensor, offset=off, ap=[[PADC, PADR], [-1, 64], [1, 64]])
                    sp.dma_start(s_toe[l, h, r].rearrange("c (r k) -> r c k", k=64), src).then_inc(toe_in, 16)
        sp.dma_start(s_ones, I["k_ones"][0:1, :]).then_inc(toe_in, 16)
        sp.wait_ge(toe_in, (DEPTH * 8 + 1) * 16)
        barrier(sp, 1)

        with sp.Fori(0, DEPTH) as l:
            sp.dma_start(mods.rearrange("p a b -> p (a b)"), s_mods[l]).then_inc(small_in, 16)
            sp.dma_start(gains[:, 0], I["norm1_g"][l].rearrange("(k p) -> p k", p=P)).then_inc(small_in, 16)
            sp.dma_start(gains[:, 1], I["norm2_g"][l].rearrange("(k p) -> p k", p=P)).then_inc(small_in, 16)
            sp.dma_start(lam_i, bass.AP(tensor=I["k_lam_init"].tensor, offset=l, ap=[[0, P], [1, 1]])
                         ).then_inc(small_in, 16)
            for i, nm in enumerate(("diff_lq1", "diff_lk1", "diff_lq2", "diff_lk2")):
                sp.dma_start(lam_v[:, i], bass.AP(tensor=I[nm].tensor, offset=l * 32, ap=[[0, P], [1, 32]])
                             ).then_inc(small_in, 16)
            sp.dma_start(sink_c, bass.AP(tensor=I["swa_sink"].tensor, offset=l * 4, ap=[[0, P], [1, 4]])
                         ).then_inc(small_in, 16)
            for hh in range(2):
                sp.dma_start(sub_g[hh * 64:hh * 64 + 64, 0:1], I["diff_subln_g"][l].rearrange("(d a) -> d a", a=1)
                             ).then_inc(a_tab, 16)

            load_unit(sp, l, 0, w_in_v[l, :, :, 0:UW])
            load_unit(sp, l, 1, w_in_v[l, :, :, UW:2 * UW])

            cache_src = {"A": I["cache_na_k"], "B": I["cache_diff_k"], "D": I["cache_swa_k"]}

            def store(g):
                if g["form"] != "n":
                    s = g["hi"] % 2
                    sp.wait_ge(zlo_rdy, l * NT + g["hi"] + 1)
                    what, kind, row = g["dst"]
                    dst = (s_q if what == "q" else s_k)[kind]
                    for part, src in ((0, z_hi[s]), (1, z_lo[s])):
                        sp.dma_start(dst[part, row:row + P, g["col"]:g["col"] + g["n"]],
                                     src[:, :g["n"]].bitcast(F32)).then_inc(z_out[s], 16)
                    return
                s = g["ni"] % 2
                sp.wait_ge(vn_rdy, l * NN + g["ni"] + 1)
                t, form = g["t"], g["nform"]
                if form != "t":
                    c0 = 768 if form == "s" else IN_UNITS[g["unit"]][2]
                    sp.dma_start(s_v[t * P:(t + 1) * P, c0:c0 + UW], vn[s]).then_inc(vn_out[s], 16)
                name = {1: "o_na_k", 2: "o_na_v", 4: "o_df_k", 5: "o_df_v"}.get(g["unit"])
                if t >= LAT // P:
                    r0 = t * P - LAT
                    if name:
                        sp.dma_start(O[name][0, l, r0:r0 + P].rearrange("t h d -> t (h d)"), vn[s]).then_inc(vn_out[s], 16)
                    if form == "s":
                        sp.dma_start(O["o_sw_k"][0, l, r0:r0 + P].rearrange("t h d -> t (h d)"), vn[s][:, 0:P]
                                     ).then_inc(vn_out[s], 16)
                        sp.dma_start(O["o_sw_v"][0, l, r0:r0 + P].rearrange("t h d -> t (h d)"), vn[s][:, P:UW]
                                     ).then_inc(vn_out[s], 16)

            for g in GROUPS:
                if g["form"] == "cache":
                    if g["i"]:
                        sp.wait_ge(z_full, l * NG + g["i"])
                    sp.dma_start(cache_n, cache_src[g["kind"]][0, l].rearrange("(t p) h d -> p t (h d)", p=P)[
                        :, :, g["row"]:g["row"] + P]).then_inc(cache_in, 16)
                if g.get("first_of_unit") and g["unit"] + 2 < NU_IN:
                    u = g["unit"] + 2
                    load_unit(sp, l, u, w_in_v[l, :, :, u * UW:(u + 1) * UW])
                if g["form"] == "rope":
                    r = g["ri"]
                    if r == 0:
                        sp.wait_ge(n_lo, l * (2 * NCH * KT) + (NCH * KT + CREDIT))
                    sp.wait_ge(rp_1, l * NR + r + 1)
                    sp.wait_ge(rp_2, l * NR + r + 1)
                    kd = 0 if g["kind"] == "B" else 1
                    sp.dma_start(rope_t[r % 2], I["k_rope"][kd, :, :, g["c"] * 512:(g["c"] + 1) * 512].rearrange(
                        "s p n -> p s n")).then_inc(rope_in[r % 2], 16)
                if g["i"] >= 1:
                    store(GROUPS[g["i"] - 1])
            store(GROUPS[-1])
            for s in range(2):
                sp.wait_ge(z_out[s], (l + 1) * T_USES[s] * 32)
                settle(sp)
                sp.wait_ge(vn_out[s], (l + 1) * N_BYTES[s])
            barrier(sp, l * PHASES + 2)

            sp.dma_start(fc_n, s_v[:, 512:768].rearrange("(t p) n -> p t n", p=P)).then_inc(f_in, 16)
            sp.dma_start(w_f, I["w_fourier"][l].rearrange("(k p) n -> p k n", p=P)).then_inc(f_in, 16)
            sp.dma_start(dft_ch, I["k_dft_ch"].rearrange("s p n -> p s n")).then_inc(f_in, 16)
            i = 0
            for c, (c0, n) in enumerate(CHUNKS):
                tab = I["k_dft_lat"] if c < 2 else I["k_dft_ctx"]
                kts = LAT // P if c < 2 else SEQ // P
                for kt in range(kts):
                    if i >= 4:
                        sp.wait_ge(dft_used, l * NDFT + i - 3)
                    cc = c0 if c < 2 else 0
                    sp.dma_start(dft_t[i % 4][:, :, :n], tab[:, kt * P:(kt + 1) * P, cc:cc + n].rearrange(
                        "s p n -> p s n")).then_inc(dft_in[i % 4], 16)
                    i += 1
                if c > 0:
                    fourier_store(sp, l, c - 1)
            fourier_store(sp, l, NCH - 1)
            for s in range(2):
                sp.wait_ge(f_out[s], (l + 1) * NCH * 32)
            barrier(sp, l * PHASES + 3)

            sp.dma_start(swa_q, I["k_swa_mask_q"]).then_inc(a_tab, 16)
            sp.dma_start(swa_k, I["k_swa_mask_k"]).then_inc(a_tab, 16)
            sp.dma_start(sink_rows, I["k_sink_rows"].rearrange("s p n -> p s n")).then_inc(a_tab, 16)
            sp.wait_ge(a_init, l + 1)

            def load_head(v):
                kind, h, half, _, _ = JOBS[v * NCH]
                b, vb = v % 2, h % 2
                if v >= 2:
                    sp.wait_ge(pv_done, l * STEPS + STEP0[(v - 1) * NCH])
                S = head_in[b]
                if kind == "B":
                    r0 = h * 64 + half * 32
                    parts_q = [(0, 0), (32, 1), (64, 0)]
                    parts_k = [(0, 0), (32, 0), (64, 1)]
                    for (row, part), (rk, pk) in zip(parts_q, parts_k):
                        sp.dma_start(q1[b][row:row + 32].bitcast(F32), s_q["B"][part, r0:r0 + 32]).then_inc(S, 16)
                        sp.dma_start(k1[b][rk:rk + 32].bitcast(F32), s_k["B"][pk, r0:r0 + 32]).then_inc(S, 16)
                    sp.dma_start(k1[b][96:97].bitcast(F32), ones_row(KEYS)).then_inc(S, 16)
                else:
                    r0 = h * 64
                    rk = h * 64 if kind == "A" else (h // 2) * 64
                    for part in range(2):
                        sp.dma_start(q1[b][part * 64:part * 64 + 64].bitcast(F32), s_q[kind][part, r0:r0 + 64]
                                     ).then_inc(S, 16)
                        sp.dma_start(k1[b][part * 64:part * 64 + 64].bitcast(F32), s_k[kind][0, rk:rk + 64]
                                     ).then_inc(S, 16)
                    sp.dma_start(q2[b][0:64].bitcast(F32), s_q[kind][0, r0:r0 + 64]).then_inc(S, 16)
                    sp.dma_start(k2[b][0:64].bitcast(F32), s_k[kind][1, rk:rk + 64]).then_inc(S, 16)
                if half == 0:
                    c0 = {"A": h * 64, "B": 256 + h * 64, "D": 896 + (h // 2) * 64}[kind]
                    cache = {"A": I["cache_na_v"], "B": I["cache_diff_v"], "D": I["cache_swa_v"]}[kind]
                    hk = h // 2 if kind == "D" else h
                    vs = slice(vb * 64, vb * 64 + 64)
                    sp.dma_start(vv[vb][:, 0:8, vs], s_v[0:LAT, c0:c0 + 64].rearrange("(t p) d -> p t d", p=P)
                                 ).then_inc(S, 16)
                    sp.dma_start(vv[vb][:, 8:12, vs], cache[0, l, :, hk].rearrange("(t p) d -> p t d", p=P)
                                 ).then_inc(S, 16)
                    sp.dma_start(vv[vb][:, 12:14, vs], s_v[LAT:TOK, c0:c0 + 64].rearrange("(t p) d -> p t d", p=P)
                                 ).then_inc(S, 16)

            nmask = [0]

            def load_masks(which):
                if which == 0:
                    srcs = [(I["k_na_mask_q"][p_], 640) for p_ in range(5)]
                else:
                    srcs = [(I["k_na_mask_k"][which - 1, k], 512) for k in range(6)]
                for src, n in srcs:
                    i = nmask[0]
                    if i >= 2:
                        sp.wait_ge(b_rdy, l * NMASK + i - 1)
                    sp.dma_start(na_m[i % 2][:, :n], src).then_inc(nm_in[i % 2], 16)
                    nmask[0] += 1

            def load_bias(h, which):
                if which == 0:
                    for pi, t in enumerate((0, 1, 2, 6, 7)):
                        for a in range(2):
                            dr = 2 * key_tile0(t) - 2 * t - a + 11
                            sp.dma_start(na_q[a * 64:a * 64 + 64, pi * 640:(pi + 1) * 640],
                                         s_toe[l, h, 0, :, dr * 64:dr * 64 + 640]).then_inc(b_in[0], 16)
                else:
                    ch = which - 1
                    for k in range(6):
                        for b in range(2):
                            r = 11 - (2 * (2 * ch + k) + b - 8 * ch)
                            sp.dma_start(na_k[ch][b * 64:b * 64 + 64, k * 512:(k + 1) * 512],
                                         s_toe[l, h, 1, :, r * 64:r * 64 + 512]).then_inc(b_in[which], 16)
                load_masks(which)

            stored = [0]

            def store_out(kind, h2, c):
                i = stored[0]
                s = i % 2
                c0, n = CHUNKS[c]
                r0 = {"A": 0, "B": 256, "D": 768}[kind] + h2 * P
                sp.wait_ge(ao_l, l * NAO + i + 1)
                for part, src in ((0, ao_hi[s]), (1, ao_lo[s])):
                    sp.dma_start(s_o[part, r0:r0 + P, c0:c0 + n], src[:, :n].bitcast(F32)).then_inc(ao_out[s], 16)
                stored[0] += 1

            load_head(0)
            for w in range(3):
                load_bias(0, w)
            for j, (kind, h, half, c, v) in enumerate(JOBS):
                if c == 0 and v + 1 < 16:
                    load_head(v + 1)
                if kind == "A" and h < 3:
                    if c == 1:
                        sp.wait_ge(s1_max, l * PIECES + PIECE0[j + 1])
                        load_bias(h + 1, 0)
                        sp.wait_ge(s2_add, l * NADD + ADD0[j])
                        load_bias(h + 1, 1)
                    if c == 2:
                        sp.wait_ge(s2_add, l * NADD + ADD0[j])
                        load_bias(h + 1, 2)
                if j >= 1:
                    pk, ph, phalf, pc, pv_ = JOBS[j - 1]
                    if j >= 2 and is_pair(j - 2):
                        store_out(JOBS[j - 2][0], JOBS[j - 2][1] // 2, JOBS[j - 2][3])
            for j in (NJ - 2, NJ - 1):
                store_out(JOBS[j][0], JOBS[j][1] // 2, JOBS[j][3])
            for h2 in range(2):
                for c in range(NCH):
                    store_out("B", h2, c)
            for s in range(2):
                sp.wait_ge(ao_out[s], (l + 1) * (NAO // 2) * 32)
            barrier(sp, l * PHASES + 4)

            n0 = NU_IN
            load_unit(sp, l, n0, w_out_v[l, :, :, 0:UW])
            for c, (c0, n) in enumerate(CHUNKS):
                for part, dst in ((0, h_hi), (1, h_lo)):
                    sp.dma_start(dst[:, :, c0:c0 + n].bitcast(F32), s_o[part, :, c0:c0 + n].rearrange(
                        "(k p) n -> p k n", p=P)).then_inc(o_in[c], 16)
            for u in range(1, NU_OUT):
                load_unit(sp, l, n0 + u, w_out_v[l, :, :, u * UW:(u + 1) * UW])

            def load_up(b):
                load_unit(sp, l, NU_IN + NU_OUT + 2 * b, w1_v[l, :, :, bass.ds(b * UW, UW)])

            def load_down(b):
                load_unit(sp, l, NU_IN + NU_OUT + 2 * b + 1, w2_v[l, :, bass.ds(b * 2, 2), :])

            load_up(0)
            load_down(0)
            with sp.Fori(0, NB // 2 - 1) as i:
                for bb in range(2):
                    load_up(i * 2 + bb + 1)
                    load_down(i * 2 + bb + 1)
            load_up(NB - 1)
            load_down(NB - 1)
            barrier(sp, l * PHASES + 5)

        for t in range(TOK // P):
            sp.wait_ge(y_ev, y_ev_at(t))
            dst = O["y_sample"][0, t * P:(t + 1) * P] if t < LAT // P else O["y_prompt"][0, t * P - LAT:(t + 1) * P - LAT]
            sp.dma_start(dst, y_nat[:, t]).then_inc(y_out, 16)
        sp.wait_ge(y_out, (TOK // P) * 16)

    SMALL0, SMALL = 20, 9

    @block.gpsimd
    def _(pool):
        pool.sem_inc(n_f, CREDIT)
        pool.sem_inc(mhi_rdy, CREDIT)
        pool.sem_inc(rp_2, CREDIT)
        barrier(pool, 1)
        with pool.Fori(0, DEPTH) as l:
            hi_unit(pool, l, 0, 0, None)
            hi_unit(pool, l, 1, 1, None)
            pool.wait_ge(mod_rdy, l * 4 + 4)
            norm_pool(pool, l * 2, lambda k, cd: mod_a[:, 0, k, cd:cd + 1], lambda k, cd: mods[:, k, cd:cd + 1])

            def turned(g):
                r = g["ri"]
                pool.wait_ge(zf_rdy, l * NR + r + 1)
                pool.wait_ge(rope_in[r % 2], l * R_USES[r % 2] * 16 + (r // 2 + 1) * 16)
                pool.wait_ge(zr_rdy, l * NR + r + 1)
                pool.tensor_tensor(rp2[r % 2], zf[r % 2], rope_t[r % 2][:, 0], ALU.mult).then_inc(rp_2, 1)

            for g in GROUPS:
                if g["i"] and GROUPS[g["i"] - 1]["form"] == "rope":
                    turned(GROUPS[g["i"] - 1])
                if g.get("first_of_unit") and g["unit"] + 2 < NU_IN:
                    u = g["unit"] + 2
                    hi_unit(pool, l, u, unit_slot(u), unit_prev(u))
            barrier(pool, l * PHASES + 2)
            barrier(pool, l * PHASES + 3)

            i = 0
            for h in range(4):
                for which in range(3):
                    per = 160 if which == 0 else 192
                    pool.wait_ge(b_in[which], l * 4 * per + (h + 1) * per)
                    for m in range(MASKS[which]):
                        n = 640 if which == 0 else 512
                        tab = (na_q if which == 0 else na_k[which - 1])[:, m * n:(m + 1) * n]
                        pool.wait_ge(nm_in[i % 2], l * (NMASK // 2) * 16 + (i // 2 + 1) * 16)
                        pool.tensor_tensor(tab, tab, na_m[i % 2][:, :n], ALU.add).then_inc(b_rdy, 1)
                        i += 1
            barrier(pool, l * PHASES + 4)

            for u in range(NU_OUT):
                n = NU_IN + u
                hi_unit(pool, l, n, unit_slot(n), unit_prev(n))
            n = NU_IN + NU_OUT
            hi_unit(pool, l, n, unit_slot(n), NU_IN)
            pool.wait_ge(q_full, l * Q_LAYER + NU_OUT * NCH * 2)
            hi_unit(pool, l, n + 1, unit_slot(n + 1), None)
            norm_pool(pool, l * 2 + 1, lambda k, cd: mod_a[:, 1, k, cd:cd + 1], lambda k, cd: mods[:, 24 + k, cd:cd + 1])

            def block_(b, bb, last):
                for c in range(NCH):
                    n_ = CHUNKS[c][1]
                    for m in range(2):
                        x = b * 6 + (c * 2 + m)
                        buf = (bb * 3 + c) % 2
                        pool.wait_ge(sqr_rdy, l * M_LAYER + x + 1 + CREDIT)
                        pool.wait_ge(q_full, l * Q_LAYER + b * (NCH * KT) + (NU_OUT * NCH * 2 + (c - 1) * KT))
                        settle(pool)
                        pool.tensor_scalar(m_hi[buf][:, m, :n_], m_f[m][:, :n_], 1.0, 0.0, ALU.mult, ALU.add
                                           ).then_inc(mhi_rdy, 1)
                    if c == 0 and not last:
                        u = NU_IN + NU_OUT + b * 2 + 2
                        hi_unit(pool, l, u, (bb + 1) % 2, u - 4)
                if not last:
                    u = NU_IN + NU_OUT + b * 2 + 3
                    hi_unit(pool, l, u, 2, u - 2)

            with pool.Fori(0, NB // 2 - 1) as i:
                for bb in range(2):
                    block_(i * 2 + bb, bb, False)
            for bb in range(2):
                block_(NB - 2 + bb, bb, bb == 1)
            barrier(pool, l * PHASES + 5)
        norm_pool(pool, 2 * DEPTH, lambda k, cd: fin_a[:, k, 0:1], lambda k, cd: zero8[:, 0:1], final=True)

    @block.scalar
    def _(act):
        act.sem_inc(ada_copied, CREDIT)
        act.sem_inc(n_std, CREDIT)
        act.sem_inc(n_hi, CREDIT)
        act.sem_inc(r_rdy, 4)
        act.wait_ge(const_in, 8 * 16)
        act.activation(cond_t[:, 0], cond, ACT.Exp, scale=-1.0).then_inc(cond_e, 1)
        with act.Fori(0, DEPTH) as l:
            for n in range(12):
                act.wait_ge(ada_rows, l * 12 + n + 1)
                act.wait_ge(ada_used, l * 12 + n + 1)
                act.activation(m_row[0:2, n % 4], bank[0:2, n % 2, :], ACT.Copy).then_inc(ada_copied, 1)
        barrier(act, 1)
        with act.Fori(0, DEPTH) as l:
            def upper(g, src):
                s = g["hi"] % 2
                if g["hi"] >= 2:
                    act.wait_ge(z_out[s], l * T_USES[s] * 32 + (g["hi"] // 2) * 32)
                act.activation(z_hi[s][:, :g["n"]], src[:, :g["n"]], ACT.Copy, scale=g.get("scale", 1.0)
                               if g["form"] != "rope" else 1.0).then_inc(zhi_rdy, 1)

            def evacuate(g):
                act.wait_ge(z_full, l * NG + g["i"] + 1)
                src = bank[:, g["i"] % 4]
                if g["form"] in ("t", "cache"):
                    upper(g, src)
                elif g["form"] == "rope":
                    r = g["ri"]
                    act.wait_ge(rp_full, l * NR + r + 1)
                    act.wait_ge(rp_2, l * NR + r + 1)
                    act.activation(zf[r % 2], src, ACT.Copy, scale=g["scale"]).then_inc(zf_rdy, 1)
                else:
                    s = g["ni"] % 2
                    if g["ni"] >= 2:
                        act.wait_ge(vn_out[s], l * N_BYTES[s] + g["stored_before"])
                    act.activation(vn[s], src[:, :UW], ACT.Copy).then_inc(vn_rdy, 1)
                if g["i"] and GROUPS[g["i"] - 1]["form"] == "rope":
                    p = GROUPS[g["i"] - 1]
                    act.wait_ge(zr_rdy, l * NR + p["ri"] + 1 + CREDIT)
                    upper(p, zr[0])

            for g in GROUPS[:5]:
                evacuate(g)
            norm_act(act, l * 2, lambda e, c: None)
            for g in GROUPS[5:]:
                evacuate(g)
            barrier(act, l * PHASES + 2)

            for c, (c0, n) in enumerate(CHUNKS):
                for m in range(2):
                    act.wait_ge(f_o, (l * NCH + c) * 2 + m + 1)
                    if c:
                        act.wait_ge(f_out[m], (l * NCH + c) * 32)
                    act.activation(ao_hi[m][:, :n], bank[:, 6 + m, :n], ACT.Copy).then_inc(f_hi, 1)
            barrier(act, l * PHASES + 3)

            act.wait_ge(lam_d, l * 5 + 2)
            act.activation(lam_s[:, 2:4], lam_s[:, 0:2], ACT.Exp).then_inc(lam_e, 1)
            act.wait_ge(a_init, l + 1)

            def max_row(j):
                kind, _, _, c, v = JOBS[j]
                c0, n = CHUNKS[c]
                r, dst = (96, q1[v % 2]) if kind == "B" else (64, q2[v % 2])
                act.wait_ge(m_rowp, l * NJ + j + 1)
                act.activation(dst[r:r + 1, c0:c0 + n], bank[r:r + 1, 7, :n], ACT.Copy, scale=-1.0).then_inc(m_rdy, 1)

            def exponentials(j, i):
                kind = JOBS[j][0]
                _, _, n, tab = key_steps(kind, JOBS[j][3])[i]
                si = STEP0[j] + i
                if si >= NP_RING:
                    act.wait_ge(pv_done, l * STEPS + si - NP_RING + 1)
                if tab is None:
                    act.wait_ge(s2_full, l * STEPS + si + 1)
                    src = bank[:, 3 + si % 2, :n]
                else:
                    a = ADD_INDEX[(j, i)]
                    act.wait_ge(s2_add, l * NADD + a + 1)
                    src = sb[a % 2][:, :n]
                act.activation(prob[si % NP_RING][:, :n], src, ACT.Exp, scale=FS if kind == "B" else 1.0
                               ).then_inc(p_rdy, 1)

            def sink_row(j):
                _, h, _, c, v = JOBS[j]
                c0, n = CHUNKS[c]
                act.wait_ge(pv_done, l * STEPS + STEP0[j])
                act.wait_ge(m_rdy, l * NJ + j + 1)
                act.activation(p_sink[64:65, :n], q2[v % 2][64:65, c0:c0 + n].bitcast(F32), ACT.Exp,
                               bias=sink_c[64:65, h:h + 1]).then_inc(sink_p, 1)

            def upper_out(idx, src, n):
                s = idx % 2
                if idx >= 2:
                    act.wait_ge(ao_out[s], l * (NAO // 2) * 32 + (idx // 2) * 32)
                act.activation(ao_hi[s][:, :n], src, ACT.Copy).then_inc(ao_h, 1)

            def upper_pair(j):
                c0, n = CHUNKS[JOBS[j][3]]
                act.wait_ge(o_free, l * NJ + j + 1)
                upper_out(PAIR_JOBS.index(j), o_ad[:, c0:c0 + n], n)

            due = False
            for slot in SLOTS:
                if slot[0] == "first":
                    max_row(0)
                elif slot[0] == "step":
                    _, j, i, _, last = slot
                    exponentials(j, i)
                    if due:
                        max_row(j + 1)
                    due = last
                    if i == 0 and JOBS[j][0] == "D":
                        sink_row(j)
                elif slot[1] and is_pair(slot[1] - 1):
                    upper_pair(slot[1] - 1)
            upper_pair(NJ - 1)
            act.wait_ge(pv_done, (l + 1) * STEPS)
            act.wait_ge(o_mul, (l + 1) * 4 * NCH)
            for x in range(2 * NCH):
                h2, c = divmod(x, NCH)
                c0, n = CHUNKS[c]
                act.activation(prob[x][:, :n], o_b[:, h2, c0:c0 + n], ACT.Square).then_inc(sn_sq, 1)
            for x in range(2 * NCH):
                n = CHUNKS[x % NCH][1]
                act.wait_ge(sn_full, l * 6 + x + 1)
                act.activation(prob[x][:, :n], bank[:, x, :n], ACT.Sqrt, bias=eps_c, scale=1.0 / HD).then_inc(sn_std, 1)
            for x in range(2 * NCH):
                n = CHUNKS[x % NCH][1]
                act.wait_ge(sn_o, l * 6 + x + 1)
                upper_out(len(PAIR_JOBS) + x, prob[x][:, :n], n)
            barrier(act, l * PHASES + 4)

            def x_at(e, c):
                e.wait_ge(q_free, l * Q_LAYER + (NU_OUT - 1) * NCH * 2 + c * 2 + 2 + CREDIT)
            norm_act(act, l * 2 + 1, x_at)

            def block_(b, bb):
                for c in range(NCH):
                    n = CHUNKS[c][1]
                    for m in range(2):
                        x = b * 6 + (c * 2 + m)
                        act.wait_ge(p1_full, l * M_LAYER + x + 1)
                        act.wait_ge(sqr_rdy, l * M_LAYER + x + 1)
                        act.activation(m_r[m][:, :n], bank[:, (bb * 6 + c * 2 + m) % 4, :n], ACT.Relu).then_inc(r_rdy, 1)

            with act.Fori(0, NB // 2 - 1) as i:
                for bb in range(2):
                    block_(i * 2 + bb, bb)
            for bb in range(2):
                block_(NB - 2 + bb, bb)
            barrier(act, l * PHASES + 5)

        def rows(c):
            n = CHUNKS[c][1]
            for k in range(KT):
                i = c * KT + k
                act.wait_ge(y_full, i + 1 + CREDIT)
                act.activation(y_nat[:, 4 * c:4 * c + n // P, k * P:(k + 1) * P],
                               bank[:, i % 4, :n].rearrange("p (t f) -> p t f", f=P), ACT.Copy).then_inc(y_ev, 1)
        norm_act(act, 2 * DEPTH, lambda e, c: None, final=rows)

    @block.vector
    def _(dve):
        dve.sem_inc(n_rs, CREDIT)
        dve.sem_inc(n_lo, CREDIT)
        dve.sem_inc(wlo_rdy, 1)
        dve.sem_inc(ada_mods, 1)
        dve.sem_inc(rp_1, CREDIT)
        dve.sem_inc(zr_rdy, CREDIT)
        dve.sem_inc(q_free, CREDIT)
        dve.sem_inc(sqr_rdy, CREDIT)
        dve.sem_inc(mlo_rdy, CREDIT)
        dve.memset(eps_c, EPS)
        dve.memset(zero8, 0.0)
        dve.memset(pad_zero, 0.0).then_inc(misc, 1)
        dve.wait_ge(cond_e, 1)
        dve.tensor_scalar(cond_t[:, 1], cond_t[:, 0], 1.0, None, ALU.add).then_inc(cond_d, 1)
        dve.wait_ge(cond_d, 1)
        dve.reciprocal(cond_t[:, 2], cond_t[:, 1]).then_inc(cond_d, 1)
        dve.wait_ge(cond_d, 2)
        dve.tensor_tensor(cond, cond, cond_t[:, 2], ALU.mult).then_inc(cond_d, 1)
        for i in range(FT):
            c, k = divmod(i, KT)
            c0, n = CHUNKS[c]
            dve.wait_ge(xt_full, i + 1)
            dve.tensor_copy(xT[:, k, c0:c0 + n], bank[:, 4 + i % 4, :n]).then_inc(xt_free, 1)
        with dve.Fori(0, DEPTH) as l:
            dve.wait_ge(ada_modp, l + 1)
            dve.wait_ge(ada_ok, l + 1)
            dve.tensor_copy(mods.rearrange("p a b -> p (a b)"), bank[:, 3, 0:96]).then_inc(ada_mods, 1)
        barrier(dve, 1)

        with dve.Fori(0, DEPTH) as l:
            dve.wait_ge(small_in, l * SMALL * 16 + (SMALL0 + SMALL) * 16)
            for w in range(2):
                for cd in range(2):
                    g0 = 8 * (3 * w + 1)
                    dve.scalar_tensor_tensor(out=mod_a[:, w, :, cd], in0=mods[:, g0:g0 + KT, cd], scalar=1.0,
                                             in1=gains[:, w], op0=ALU.add, op1=ALU.mult).then_inc(mod_rdy, 1)
            dve.tensor_tensor_reduce(rp1[:, 0:32], lam_v[:, 0], lam_v[:, 1], 1.0, 0.0, ALU.mult, ALU.add,
                                     lam_s[:, 0:1]).then_inc(lam_d, 1)
            dve.tensor_tensor_reduce(rp1[:, 32:64], lam_v[:, 2], lam_v[:, 3], 1.0, 0.0, ALU.mult, ALU.add,
                                     lam_s[:, 1:2]).then_inc(lam_d, 1)

            def lower(g, src, scale):
                s = g["hi"] % 2
                n = g["n"]
                dve.wait_ge(zhi_rdy, l * NT + g["hi"] + 1)
                dve.scalar_tensor_tensor(out=z_lo[s][:, :n], in0=src[:, :n], scalar=scale, in1=z_hi[s][:, :n].bitcast(F32),
                                         op0=ALU.mult, op1=ALU.subtract).then_inc(zlo_rdy, 1)

            def evacuate(g):
                if g["form"] in ("t", "cache"):
                    lower(g, bank[:, g["i"] % 4], g.get("scale", 1.0))
                if g["i"] and GROUPS[g["i"] - 1]["form"] == "rope":
                    p = GROUPS[g["i"] - 1]
                    r = p["ri"]
                    dve.wait_ge(rp_full, l * NR + r + 1 + CREDIT)
                    dve.wait_ge(rope_in[r % 2], l * R_USES[r % 2] * 16 + (r // 2 + 1) * 16)
                    dve.tensor_tensor(rp1, bank[:, 4 + r % 2], rope_t[r % 2][:, 1], ALU.mult).then_inc(rp_1, 1)
                    dve.wait_ge(rp_1, l * NR + r + 1 + CREDIT)
                    dve.wait_ge(rp_2, l * NR + r + 1 + CREDIT)
                    dve.tensor_tensor(zr[0], rp1, rp2[r % 2], ALU.add).then_inc(zr_rdy, 1)
                    lower(p, zr[0], 1.0)
                if g.get("fourth_of_unit") and g["unit"] + 2 < NU_IN:
                    lo_unit(dve, l, g["unit"] + 2, unit_slot(g["unit"] + 2))

            lo_unit(dve, l, 0, 0)
            lo_unit(dve, l, 1, 1)
            for g in GROUPS[:5]:
                evacuate(g)
            norm_dve(dve, l * 2)
            for g in GROUPS[5:]:
                evacuate(g)
            barrier(dve, l * PHASES + 2)

            for m in range(2):
                dve.wait_ge(f_gp, l + 1)
                dve.tensor_copy(g_cs[:, m], bank[:, m].rearrange("p (s n) -> p s n", s=2)).then_inc(f_g, 1)
            for c, (c0, n) in enumerate(CHUNKS):
                dve.wait_ge(f_full, l * NCH + c + 1)
                if c:
                    dve.wait_ge(f_o, (l * NCH + c) * 2)
                for x in range(4):
                    dve.tensor_copy(f_ab[:, x, :n], bank[:, 2 + x, :n]).then_inc(f_ev, 1)
                for m in range(2):
                    dve.wait_ge(f_hi, (l * NCH + c) * 2 + m + 1)
                    dve.tensor_tensor(ao_lo[m][:, :n], bank[:, 6 + m, :n], ao_hi[m][:, :n].bitcast(F32), ALU.subtract
                                      ).then_inc(f_lo, 1)
            barrier(dve, l * PHASES + 3)

            for b in range(2):
                dve.memset(q2[b][64:96].bitcast(F32), 0.0)
                dve.memset(k2[b][64:96].bitcast(F32), 1.0)
                dve.memset(vv[b][:, :, 64 * (1 - b):64 * (1 - b) + 64], 1.0)
            dve.memset(p_sink, 0.0).then_inc(a_init, 1)
            dve.wait_ge(lam_e, l + 1)
            dve.wait_ge(a_tab, l * 80 + 80)
            dve.tensor_tensor(lam_s[:, 4:5], lam_s[:, 3:4], lam_s[:, 2:3], ALU.subtract).then_inc(lam_d, 1)
            dve.tensor_scalar(lam_s[:, 6:7], lam_i, -1.0, 1.0, ALU.mult, ALU.add).then_inc(lam_d, 1)
            dve.wait_ge(lam_d, l * 5 + 4)
            dve.tensor_tensor(lam_s[:, 5:6], lam_s[:, 4:5], lam_i, ALU.subtract)
            dve.tensor_tensor(sub_g[:, 1:2], sub_g[:, 0:1], lam_s[:, 6:7], ALU.mult).then_inc(lam_d, 1)
            dve.wait_ge(lam_d, l * 5 + 5)

            def table_ready(kind, h, which):
                if kind == "A":
                    dve.wait_ge(b_rdy, l * NMASK + h * sum(MASKS) + sum(MASKS[:which + 1]))

            def piece(j, p):
                kind, h, _, c, v = JOBS[j]
                t, x, _, n, tab = row_pieces(kind, c)[p]
                gi = PIECE0[j] + p
                np_ = len({q[1] for q in row_pieces(kind, c)})
                if kind == "D" and p == 0:
                    nt = CHUNKS[c][1] // P
                    dve.tensor_scalar(mp[:, 0:nt, np_], zero8[:, 0:nt], sink_c[:, h:h + 1], None, ALU.add)
                dve.wait_ge(s1_full, l * PIECES + gi + 1)
                src = bank[:, gi % 3, :n]
                if tab is None:
                    dve.tensor_reduce(mp[:, t, x:x + 1], src, AX.X, ALU.max).then_inc(s1_max, 1)
                else:
                    table_ready(kind, h, 0)
                    table = (na_q if kind == "A" else swa_q)[:, tab:tab + n]
                    if gi >= 2:
                        dve.wait_ge(s1_max, l * PIECES + gi - 1)
                    settle(dve)
                    dve.tensor_tensor_reduce(junk[:, gi % 2, :n], src, table, 1.0, 3.0 * NEG, ALU.add, ALU.max,
                                             mp[:, t, x:x + 1]).then_inc(s1_max, 1)

            def maxima(j):
                kind, _, _, c, _ = JOBS[j]
                nt = CHUNKS[c][1] // P
                np_ = len({q[1] for q in row_pieces(kind, c)}) + (kind == "D")
                dve.wait_ge(s1_max, l * PIECES + PIECE0[j + 1])
                if j >= 2:
                    dve.wait_ge(m_rowp, l * NJ + j - 1)
                dve.tensor_reduce(mcol[j % 2][:, 0:nt], mp[:, 0:nt, 0:np_], AX.X, ALU.max).then_inc(m_col, 1)

            def add_bias(j, i):
                kind, h, _, c, _ = JOBS[j]
                _, _, n, tab = key_steps(kind, c)[i]
                a, si = ADD_INDEX[(j, i)], STEP0[j] + i
                dve.wait_ge(s2_full, l * STEPS + si + 1)
                table_ready(kind, h, 1 + c)
                if a >= 2:
                    pj, pi = ADDS[a - 2]
                    dve.wait_ge(p_rdy, l * STEPS + STEP0[pj] + pi + 1)
                table = (na_k[c] if kind == "A" else swa_k)[:, tab:tab + n]
                dve.tensor_tensor(sb[a % 2][:, :n], bank[:, 3 + si % 2, :n], table, ALU.add).then_inc(s2_add, 1)

            nb = [0]

            def finish(j):
                kind, h, half, c, _ = JOBS[j]
                c0, n = CHUNKS[c]
                o = slice(64 * (h % 2), 64 * (h % 2) + 64)
                d = slice(64 - 64 * (h % 2), 128 - 64 * (h % 2))
                ob = bank[:, 5 + j % 2, :n]
                dve.wait_ge(pv_done, l * STEPS + STEP0[j + 1])
                dve.reciprocal(rden[o, :n], ob[d]).then_inc(o_den, 1)
                dve.wait_ge(o_den, l * NJ + j + 1)
                if kind != "B":
                    earlier = [i for i, p in enumerate(PAIR_JOBS) if p < j - 2 and JOBS[p][3] == c]
                    if earlier:
                        dve.wait_ge(ao_h, l * NAO + earlier[-1] + 1)
                    dve.tensor_tensor(o_ad[o, c0:c0 + n], ob[o], rden[o, :n], ALU.mult).then_inc(o_free, 1)
                    return
                dst = o_b[o, h // 2, c0:c0 + n] if half == 0 else o_t[o, :n]
                dve.tensor_tensor(dst, ob[o], rden[o, :n], ALU.mult).then_inc(o_free, 1)
                if half:
                    dve.wait_ge(o_free, l * NJ + j + 1)
                    dst = o_b[o, h // 2, c0:c0 + n]
                    dve.scalar_tensor_tensor(out=dst, in0=o_t[o, :n], scalar=lam_s[o, 5:6], in1=dst, op0=ALU.mult,
                                             op1=ALU.add).then_inc(o_mul, 1)

            def lower_out(idx, src, n):
                dve.wait_ge(ao_h, l * NAO + idx + 1)
                dve.tensor_tensor(ao_lo[idx % 2][:, :n], src, ao_hi[idx % 2][:, :n].bitcast(F32), ALU.subtract
                                  ).then_inc(ao_l, 1)

            def lower_pair(j):
                c0, n = CHUNKS[JOBS[j][3]]
                lower_out(PAIR_JOBS.index(j), o_ad[:, c0:c0 + n], n)

            for slot in SLOTS:
                if slot[0] == "first":
                    for p in slot[2]:
                        piece(0, p)
                    maxima(0)
                elif slot[0] == "step":
                    _, j, i, now, last = slot
                    if (j, i) in ADD_INDEX:
                        add_bias(j, i)
                    for p in now:
                        piece(j + 1, p)
                    if last:
                        maxima(j + 1)
                    if i == 1 and j:
                        finish(j - 1)
                elif slot[1] and is_pair(slot[1] - 1):
                    lower_pair(slot[1] - 1)
            finish(NJ - 1)
            lower_pair(NJ - 1)
            for x in range(2 * NCH):
                h2, c = divmod(x, NCH)
                c0, n = CHUNKS[c]
                dve.wait_ge(sn_std, l * 6 + x + 1)
                dve.reciprocal(rden[:, :n], prob[x][:, :n]).then_inc(sn_r, 1)
                dve.wait_ge(sn_r, l * 6 + x + 1)
                dve.scalar_tensor_tensor(out=prob[x][:, :n], in0=o_b[:, h2, c0:c0 + n], scalar=sub_g[:, 1:2],
                                         in1=rden[:, :n], op0=ALU.mult, op1=ALU.mult).then_inc(sn_o, 1)
                lower_out(len(PAIR_JOBS) + x, prob[x][:, :n], n)
            barrier(dve, l * PHASES + 4)

            def residual(l, gate, q, bk, k, c):
                c0, n = CHUNKS[c]
                cd = 1 if c == 2 else 0
                dve.wait_ge(q_full, q + 1)
                x = xT[:, k, c0:c0 + n]
                dve.scalar_tensor_tensor(out=x, in0=bank[:, bk, :n], scalar=mods[:, gate + k, cd:cd + 1], in1=x,
                                         op0=ALU.mult, op1=ALU.add).then_inc(q_free, 1)

            for u in range(3):
                lo_unit(dve, l, NU_IN + u, unit_slot(NU_IN + u))
            for u in range(NU_OUT):
                for c in range(NCH):
                    for m in range(2):
                        q = (u * NCH + c) * 2 + m
                        residual(l, 16, l * Q_LAYER + q, 4 + q % 2, 2 * u + m, c)
                if u >= 1:
                    lo_unit(dve, l, NU_IN + u + 2, unit_slot(NU_IN + u + 2))
            norm_dve(dve, l * 2 + 1)

            def block_(b, bb, last):
                def hidden(c):
                    n = CHUNKS[c][1]
                    for m in range(2):
                        x = b * 6 + (c * 2 + m)
                        buf = (bb * 3 + c) % 2
                        dve.wait_ge(r_rdy, l * M_LAYER + x + 1 + 4)
                        dve.wait_ge(mhi_rdy, l * M_LAYER + x + 1)
                        dve.wait_ge(mlo_rdy, l * M_LAYER + x + 1)
                        dve.tensor_tensor(m_f[m][:, :n], m_r[m][:, :n], m_r[m][:, :n], ALU.mult).then_inc(sqr_rdy, 1)
                    for m in range(2):
                        x = b * 6 + (c * 2 + m)
                        dve.wait_ge(mhi_rdy, l * M_LAYER + x + 1 + CREDIT)
                        dve.tensor_tensor(m_lo[buf][:, m, :n], m_f[m][:, :n], m_hi[buf][:, m, :n].bitcast(F32),
                                          ALU.subtract).then_inc(mlo_rdy, 1)

                def down(c):
                    for k in range(KT):
                        q = b * (NCH * KT) + (NU_OUT * NCH * 2 + c * KT + k)
                        residual(l, 40, l * Q_LAYER + q, 4 + k % 2, k, c)

                hidden(0)
                if not last:
                    lo_unit(dve, l, NU_IN + NU_OUT + b * 2 + 2, (bb + 1) % 2)
                hidden(1)
                down(0)
                hidden(2)
                down(1)
                down(2)
                if not last:
                    lo_unit(dve, l, NU_IN + NU_OUT + b * 2 + 3, 2)

            with dve.Fori(0, NB // 2 - 1) as i:
                for bb in range(2):
                    block_(i * 2 + bb, bb, False)
            for bb in range(2):
                block_(NB - 2 + bb, bb, bb == 1)
            barrier(dve, l * PHASES + 5)
        norm_dve(dve, 2 * DEPTH, final=True)

    @block.tensor
    def _(pe):
        pe.sem_inc(ada_used, 4)
        pe.sem_inc(n_squ, CREDIT)
        pe.sem_inc(rp_full, CREDIT)
        pe.sem_inc(y_full, CREDIT)
        pe.wait_ge(const_in, 8 * 16)
        pe.wait_ge(xin, (TOK // P) * 16)
        for i in range(FT):
            c, k = divmod(i, KT)
            if i >= 4:
                pe.wait_ge(xt_free, i - 3)
            nt = CHUNKS[c][1] // P
            for t in range(nt):
                mm = pe.transpose(bank[:, 4 + i % 4, t * P:(t + 1) * P], x_nat[:, 4 * c + t, k * P:(k + 1) * P], ident)
            mm.then_inc(xt_full, 1)
        pe.wait_ge(cond_d, 3)
        with pe.Fori(0, DEPTH) as l:
            def columns(n):
                pe.wait_ge(ada_copied, l * 12 + n + 1 + CREDIT)
                if n == 0:
                    pe.wait_ge(ada_mods, l + 1)
                for j in range(4):
                    x = (n * 4 + j) * 2
                    mm = pe.matmul(bank[:, 3, x:x + 2], m_row[0:3, n % 4, j * P:(j + 1) * P], pair, start=True, stop=True)
                    if j == 3 and n < 11:
                        mm.then_inc(ada_used, 1)
                return mm
            for n in range(12):
                pe.wait_ge(ada_in[n % 4], l * 96 + (n // 4 + 1) * 32)
                pe.wait_ge(ada_copied, l * 12 + n + 1)
                for k in range(KT):
                    mm = pe.matmul(bank[0:2, n % 2, :], cond[:, k], ada_w[n % 4][:, k], start=(k == 0), stop=(k == KT - 1))
                mm.then_inc(ada_rows, 1)
                if n:
                    columns(n - 1)
            columns(11).then_inc(ada_modp, 1)
            pe.wait_ge(ada_modp, l + 1)
            pe.sem_inc(ada_used, 1)
        barrier(pe, 1)

        def three(out, a_hi, a_lo, b_hi, b_lo, first, last):
            x = pe.matmul(out, a_hi, b_hi, start=first, stop=False)
            pe.matmul(out, a_hi, b_lo, start=False, stop=False)
            return x, pe.matmul(out, a_lo, b_hi, start=False, stop=last)

        with pe.Fori(0, DEPTH) as l:
            def in_group(g):
                i = g["i"]
                if i >= 4:
                    p = GROUPS[i - 4]
                    if p["form"] == "rope":
                        pe.wait_ge(zf_rdy, l * NR + p["ri"] + 1)
                    elif p["form"] == "n":
                        pe.wait_ge(vn_rdy, l * NN + p["ni"] + 1)
                    else:
                        pe.wait_ge(zlo_rdy, l * NT + p["hi"] + 1)
                out = bank[:, i % 4, :g["n"]]
                if g["form"] == "cache":
                    pe.wait_ge(cache_in, l * 80 + (i + 1) * 16)
                    for t in range(4):
                        mm = pe.transpose(out[:, t * P:(t + 1) * P], cache_n[:, t], ident)
                    mm.then_inc(z_full, 1)
                    return
                u = g["unit"]
                if g.get("first_of_unit"):
                    pe.wait_ge(wlo_rdy, l * U_LAYER + u + 1 + 1)
                s = unit_slot(u)
                for k in range(KT):
                    if g["form"] == "n":
                        t = slice(g["t"] * P, (g["t"] + 1) * P)
                        w = slice(k * UW, (k + 1) * UW)
                        x, mm = three(out, h_hi[:, k, t], h_lo[:, k, t], w_hi[s][:, w], w_lo[s][:, w], k == 0, k == KT - 1)
                    else:
                        w = slice(k * UW + g["m"] * P, k * UW + (g["m"] + 1) * P)
                        c0, n = CHUNKS[g["c"]]
                        t = slice(c0, c0 + n)
                        x, mm = three(out, w_hi[s][:, w], w_lo[s][:, w], h_hi[:, k, t], h_lo[:, k, t], k == 0, k == KT - 1)
                    if k == 0 and g.get("first_of_unit"):
                        x.then_inc(w_used, 1)
                mm.then_inc(z_full, 1)

            def swapped(g):
                r = g["ri"]
                pe.wait_ge(zf_rdy, l * NR + r + 1)
                pe.wait_ge(rp_1, l * NR + r + 1)
                pe.matmul(bank[:, 4 + r % 2], swap[:, 0 if g["kind"] == "B" else 1], zf[r % 2], start=True, stop=True
                          ).then_inc(rp_full, 1)

            for g in GROUPS[:5]:
                in_group(g)
            norm_pe(pe, l * 2, 0)
            norm_pe(pe, l * 2, 1)
            for g in GROUPS[5:]:
                if g["unit"] == 0 and g["m"] == 0:
                    if g["c"] == 1:
                        norm_pe(pe, l * 2, 2)
                    pe.wait_ge(n_lo, (l * 2 * NCH + g["c"] + 1) * KT + CREDIT)
                in_group(g)
                if GROUPS[g["i"] - 1]["form"] == "rope":
                    swapped(GROUPS[g["i"] - 1])
            barrier(pe, l * PHASES + 2)

            pe.wait_ge(f_in, (l + 1) * 48)
            for m in range(2):
                for s in range(2):
                    mm = pe.matmul(bank[:, m, s * 256:(s + 1) * 256], dft_ch[:, s], w_f[:, m], start=True, stop=True)
            mm.then_inc(f_gp, 1)
            i = 0
            for c, (c0, n) in enumerate(CHUNKS):
                if c:
                    pe.wait_ge(f_ev, (l * NCH + c) * 4)
                kts = LAT // P if c < 2 else SEQ // P
                for kt in range(kts):
                    s = i % 4
                    pe.wait_ge(dft_in[s], l * DFT_USES[s] * 16 + (i // 4 + 1) * 16)
                    for m in range(2):
                        for cs in range(2):
                            mm = pe.matmul(bank[:, 2 + m * 2 + cs, :n], fc_n[:, kt + (8 if c == 2 else 0), m * P:(m + 1) * P],
                                           dft_t[s][:, cs, :n], start=(kt == 0), stop=(kt == kts - 1))
                    if kt < kts - 1:
                        mm.then_inc(dft_used, 1)
                    i += 1
                mm.then_inc(f_full, 1)
                pe.wait_ge(f_full, l * NCH + c + 1)
                pe.sem_inc(dft_used, 1)
                pe.wait_ge(f_ev, (l * NCH + c + 1) * 4)
                pe.wait_ge(f_g, (l + 1) * 2)
                if c:
                    pe.wait_ge(f_lo, (l * NCH + c) * 2)
                for m2 in range(2):
                    for x in range(4):
                        mm = pe.matmul(bank[:, 6 + m2, :n], g_cs[:, x // 2, x % 2, m2 * P:(m2 + 1) * P], f_ab[:, x, :n],
                                       start=(x == 0), stop=(x == 3))
                    mm.then_inc(f_o, 1)
            barrier(pe, l * PHASES + 3)

            pe.wait_ge(a_init, l + 1)
            pe.wait_ge(a_tab, l * 80 + 80)

            def piece(j, p):
                kind, _, _, c, v = JOBS[j]
                t, _, key0, n, _ = row_pieces(kind, c)[p]
                gi = PIECE0[j] + p
                if c == 0 and p == 0:
                    pe.wait_ge(head_in[v % 2], l * HEAD_ALL[v % 2] + HEAD_IN[v])
                if gi >= 3:
                    pe.wait_ge(s1_max, l * PIECES + gi - 2)
                q0 = CHUNKS[c][0] + t * P
                rows = 96 if kind == "B" else P
                pe.matmul(bank[:, gi % 3, :n], q1[v % 2][0:rows, q0:q0 + P], k1[v % 2][0:rows, key0:key0 + n],
                          start=True, stop=True).then_inc(s1_full, 1)

            def max_row(j):
                kind, _, _, c, _ = JOBS[j]
                r = 96 if kind == "B" else 64
                pe.wait_ge(m_col, l * NJ + j + 1)
                if j:
                    pe.wait_ge(m_rdy, l * NJ + j)
                for t in range(CHUNKS[c][1] // P):
                    mm = pe.matmul(bank[r:r + 1, 7, t * P:(t + 1) * P], mcol[j % 2][:, t:t + 1], ident, start=True, stop=True)
                mm.then_inc(m_rowp, 1)

            def scores(j, i):
                kind, _, _, c, v = JOBS[j]
                key0, q0, n, _ = key_steps(kind, c)[i]
                si = STEP0[j] + i
                if i == 0:
                    pe.wait_ge(m_rdy, l * NJ + j + 1)
                if si >= 2:
                    pe.wait_ge(p_rdy, l * STEPS + si - 1)
                q = slice(CHUNKS[c][0] + q0, CHUNKS[c][0] + q0 + n)
                k = slice(key0, key0 + P)
                out = bank[:, 3 + si % 2, :n]
                b = v % 2
                if kind == "B":
                    mm = pe.matmul(out, k1[b][0:97, k], q1[b][0:97, q], start=True, stop=True)
                else:
                    pe.matmul(out, k1[b][:, k], q1[b][:, q], start=True, stop=False)
                    mm = pe.matmul(out, k2[b][:, k], q2[b][:, q], start=False, stop=True)
                mm.then_inc(s2_full, 1)

            def values(j, i):
                kind, h, _, c, v = JOBS[j]
                steps = key_steps(kind, c)
                key0, q0, n, _ = steps[i]
                si = STEP0[j] + i
                ob = bank[:, 5 + j % 2]
                if i == 0 and j >= 2:
                    pe.wait_ge(o_free, l * NJ + j - 1)
                if i == 0 and kind == "D":
                    d = sum(1 for x in JOBS[:j] if x[0] == "D")
                    pe.wait_ge(sink_p, l * 4 * NCH + d + 1)
                    nn = CHUNKS[c][1]
                    pe.matmul(ob[:, :nn], sink_rows[:, h % 2], p_sink[:, :nn], start=True, stop=False)
                pe.wait_ge(p_rdy, l * STEPS + si + 1)
                pe.matmul(ob[:, q0:q0 + n], vv[h % 2][:, key0 // P], prob[si % NP_RING][:, :n],
                          start=(i == 0 and kind != "D"), stop=(i == len(steps) - 1)).then_inc(pv_done, 1)

            due = False
            for slot in SLOTS:
                if slot[0] == "first":
                    for p in slot[2]:
                        piece(0, p)
                    max_row(0)
                elif slot[0] == "step":
                    _, j, i, now, last = slot
                    scores(j, i)
                    for p in now:
                        piece(j + 1, p)
                    if due:
                        max_row(j + 1)
                    due = last
                    if i:
                        values(j, i - 1)
                else:
                    values(slot[1], n_steps(slot[1]) - 1)
            pe.wait_ge(o_free, (l + 1) * NJ)
            for x in range(2 * NCH):
                n = CHUNKS[x % NCH][1]
                pe.wait_ge(sn_sq, l * 6 + x + 1)
                pe.matmul(bank[:, x, :n], headsum, prob[x][:, :n], start=True, stop=True).then_inc(sn_full, 1)
            barrier(pe, l * PHASES + 4)

            for u in range(NU_OUT):
                s = unit_slot(NU_IN + u)
                pe.wait_ge(wlo_rdy, l * U_LAYER + NU_IN + u + 1 + 1)
                for c, (c0, n) in enumerate(CHUNKS):
                    if u == 0:
                        pe.wait_ge(o_in[c], (l + 1) * 32)
                    for m in range(2):
                        q = (u * NCH + c) * 2 + m
                        pe.wait_ge(q_free, l * Q_LAYER + q + 1)
                        for k in range(KT):
                            w = slice(k * UW + m * P, k * UW + (m + 1) * P)
                            x, mm = three(bank[:, 4 + q % 2, :n], w_hi[s][:, w], w_lo[s][:, w], h_hi[:, k, c0:c0 + n],
                                          h_lo[:, k, c0:c0 + n], k == 0, k == KT - 1)
                            if k == 0 and c == 0 and m == 0:
                                x.then_inc(w_used, 1)
                        mm.then_inc(q_full, 1)
            for c in range(NCH):
                norm_pe(pe, l * 2 + 1, c)

            def block_(b, bb):
                def up(c):
                    c0, n = CHUNKS[c]
                    s = bb
                    if c == 0:
                        pe.wait_ge(wlo_rdy, l * U_LAYER + b * 2 + (NU_IN + NU_OUT + 1 + 1))
                    pe.wait_ge(n_lo, l * (2 * NCH * KT) + ((NCH + c + 1) * KT + CREDIT))
                    for m in range(2):
                        bk = (bb * 6 + c * 2 + m) % 4
                        x_ = b * 6 + (c * 2 + m)
                        pe.wait_ge(r_rdy, l * M_LAYER + x_ + 1)
                        for k in range(KT):
                            w = slice(k * UW + m * P, k * UW + (m + 1) * P)
                            x, mm = three(bank[:, bk, :n], w_hi[s][:, w], w_lo[s][:, w], h_hi[:, k, c0:c0 + n],
                                          h_lo[:, k, c0:c0 + n], k == 0, k == KT - 1)
                            if k == 0 and c == 0 and m == 0:
                                x.then_inc(w_used, 1)
                        mm.then_inc(p1_full, 1)

                def down(c):
                    n = CHUNKS[c][1]
                    buf = (bb * 3 + c) % 2
                    if c == 0:
                        pe.wait_ge(wlo_rdy, l * U_LAYER + b * 2 + (NU_IN + NU_OUT + 2 + 1))
                    pe.wait_ge(mlo_rdy, l * M_LAYER + b * 6 + (c + 1) * 2 + CREDIT)
                    for k in range(KT):
                        q = b * (NCH * KT) + (NU_OUT * NCH * 2 + c * KT + k)
                        pe.wait_ge(q_free, l * Q_LAYER + q + 1)
                        for f in range(2):
                            w = slice(f * D + k * P, f * D + (k + 1) * P)
                            x, mm = three(bank[:, 4 + k % 2, :n], w_hi[2][:, w], w_lo[2][:, w], m_hi[buf][:, f, :n],
                                          m_lo[buf][:, f, :n], f == 0, f == 1)
                            if k == 0 and f == 0 and c == 1:
                                x.then_inc(w_used, 1)
                        mm.then_inc(q_full, 1)

                up(0)
                up(1)
                down(0)
                up(2)
                down(1)
                down(2)

            with pe.Fori(0, NB // 2) as i:
                for bb in range(2):
                    block_(i * 2 + bb, bb)
            barrier(pe, l * PHASES + 5)

        def rows(c):
            for k in range(KT):
                i = c * KT + k
                pe.wait_ge(n_f, (2 * DEPTH * NCH + c) * KT + k + 1 + CREDIT)
                if i >= 4:
                    pe.wait_ge(y_ev, i - 3)
                for t in range(CHUNKS[c][1] // P):
                    mm = pe.transpose(bank[:, i % 4, t * P:(t + 1) * P], hf[k % 2][:, t * P:(t + 1) * P], ident)
                mm.then_inc(y_full, 1)

        norm_pe(pe, 2 * DEPTH, 0)
        for c in range(NCH):
            if c + 1 < NCH:
                norm_pe(pe, 2 * DEPTH, c + 1)
            rows(c)


_INS = ["x_prompt", "x_sample", "cache_na_k", "cache_na_v", "cache_diff_k", "cache_diff_v", "cache_swa_k", "cache_swa_v",
        "c", "c_ctx", "w_ada", "b_ada", "norm1_g", "norm2_g", "w_in", "na_rpb", "diff_lq1", "diff_lk1", "diff_lq2",
        "diff_lk2", "diff_subln_g", "w_fourier", "swa_sink", "w_out", "w_mlp1", "w_mlp2", "final_g"]
_OUTS = [("y_prompt", (1, SEQ, D)), ("y_sample", (1, LAT, D)), ("o_na_k", (1, DEPTH, SEQ, 4, HD)),
         ("o_na_v", (1, DEPTH, SEQ, 4, HD)), ("o_df_k", (1, DEPTH, SEQ, 4, HD)), ("o_df_v", (1, DEPTH, SEQ, 4, HD)),
         ("o_sw_k", (1, DEPTH, SEQ, 2, HD)), ("o_sw_v", (1, DEPTH, SEQ, 2, HD))]


def kernel(**inputs):
    import concourse.bacc as bacc
    from concourse.bass_utils import run_bass_kernel_spmd as run

    nc = bacc.Bacc("TRN2", target_bir_lowering=False, num_devices=1, dynamic_dma_scratch_size=1024)
    arrays = {n: np.ascontiguousarray(inputs[n]) for n in _INS}
    arrays["na_rpb_rev"] = np.ascontiguousarray(arrays["na_rpb"][..., ::-1, ::-1])
    arrays.update({"k_" + n: a for n, a in CONST.items()})
    I = {n: nc.dram_tensor("in_" + n, a.shape, F32, kind="ExternalInput").ap() for n, a in arrays.items()}
    O = {n: nc.dram_tensor("out_" + n, shape, F32, kind="ExternalOutput").ap() for n, shape in _OUTS}
    trunk(nc, I, O)
    r = run(nc, [{"in_" + n: a for n, a in arrays.items()}], core_ids=[0])
    return tuple(r.results[0]["out_" + n] for n, _ in _OUTS)
```

```python
import math
from contextlib import ExitStack

import numpy as np

import concourse.bass as bass
from concourse import mybir

F32 = mybir.dt.float32
F32R = mybir.dt.float32r
ALU = mybir.AluOpType
ACT = mybir.ActivationFunctionType
AX = mybir.AxisListType

P = 128
D = 1024
KT = D // P
SEQ, LAT, PAST, DEPTH = 256, 1024, 512, 2
TOK = LAT + SEQ
KEYS = LAT + PAST + SEQ
GRID_W, NA_KH, NA_KW = 64, 8, 16
ROWS = LAT // GRID_W
HD = 64
W_IN = 2304
D_FF = 4096
EPS = 1e-6
NEG = -1e30
ROPE_BASE = 10000.0
CHUNKS = [(0, 512), (512, 512), (1024, 256)]
NCH = len(CHUNKS)
UW = 256
FS = float(32) ** -0.5
QS = float(HD) ** -0.5

NU_IN, NU_OUT, NB = W_IN // UW, D // UW, D_FF // UW
U_LAYER = NU_IN + NU_OUT + 2 * NB
IN_UNITS = [("t", "A", "q"), ("t", "A", "k"), ("n", "na_v", 0), ("t", "B", "q"), ("t", "B", "k"), ("n", "df_v", 256),
            ("n", "fc", 512), ("t", "D", "q"), ("s", "D", "k")]
BR, BC = 2 * NA_KH - 1, 2 * NA_KW - 1
CREDIT = 2


def row_window(r):
    return min(max(r - NA_KH // 2, 0), ROWS - NA_KH)


def key_tile0(t):
    return min(max(t - 2, 0), ROWS // 2 - 5)


def constants():
    c = {}
    eye = np.eye(P, dtype=np.float32)
    i = np.arange(P)
    c["ident"] = eye
    c["ones"] = np.ones((P, KEYS), np.float32)
    c["headsum"] = (i[:, None] // HD == i[None, :] // HD).astype(np.float32)
    c["swap"] = np.stack([(i[:, None] == (i[None, :] ^ 8)), (i[:, None] == (i[None, :] ^ 16))]).astype(np.float32)
    ang = 2.0 * np.pi * np.outer(np.arange(HD), np.arange(HD)) / HD
    blk = np.kron(np.eye(2), np.cos(ang)), np.kron(np.eye(2), -np.sin(ang))
    c["dft_ch"] = np.stack(blk).astype(np.float32)
    for name, n in (("lat", LAT), ("ctx", SEQ)):
        a = 2.0 * np.pi * (np.outer(np.arange(n), np.arange(n)) % n) / n
        c["dft_" + name] = np.stack([np.cos(a), np.sin(a)]).astype(np.float32) / np.float32(math.sqrt(n * HD))
    rope = np.zeros((2, 2, P, LAT), np.float32)
    t = np.arange(LAT)
    for kind, d in enumerate((32, HD)):
        n = d // 2
        half = n // 2
        inv = np.float32(ROPE_BASE) ** (-np.arange(half, dtype=np.float32) / np.float32(half))
        for r in range(P):
            j = r % d
            pos = (t // GRID_W) if j < n else (t % GRID_W)
            a = pos.astype(np.float32) * inv[j % half]
            rope[kind, 0, r] = np.cos(a)
            rope[kind, 1, r] = np.sin(a) * (-1.0 if j % n < half else 1.0)
    c["rope"] = rope
    c["neg"] = np.full((P, BR * GRID_W), NEG, np.float32)
    q, k = i[:, None], i[None, :]
    prev, nxt = np.where(k >= q, 0.0, NEG), np.where(k <= q, 0.0, NEG)
    c["swa_mask_q"] = np.concatenate([prev, np.zeros((P, P)), nxt], 1).astype(np.float32)
    c["swa_mask_k"] = np.concatenate([nxt.T, np.zeros((P, P)), prev.T], 1).astype(np.float32)
    sel = np.zeros((2, P, P), np.float32)
    sel[0, 64, 64:] = 1.0
    sel[1, 64, :64] = 1.0
    c["sink_rows"] = sel
    c["lam_init"] = np.array([0.8 - 0.6 * math.exp(-0.3 * l) for l in range(DEPTH)], np.float32)
    c["pair"] = np.array([[1, 0], [0, 1], [1, 1]], np.float32)
    return c


CONST = constants()


def na_pattern(t):
    return {0: 0, 1: 1, 6: 3, 7: 4}.get(t, 2)


def attention_jobs():
    jobs, v = [], 0
    for kind, heads in (("B", [(h, s) for h in range(4) for s in range(2)]), ("A", [(h, 0) for h in range(4)]),
                        ("D", [(h, 0) for h in range(4)])):
        for h, s in heads:
            for c in range(NCH):
                jobs.append((kind, h, s, c, v))
            v += 1
    return jobs


def row_pieces(kind, c):
    out = []
    if c == 2:
        return [(t, 0, LAT + PAST, SEQ, None) for t in range(2)]
    for t in range(4):
        tt = 4 * c + t
        if kind == "B":
            out += [(t, s, 512 * s, 512, None) for s in range(3)]
        elif kind == "A":
            k0 = key_tile0(tt) * P
            out += [(t, s, k0 + 320 * s, 320, (na_pattern(tt) * 640 + 320 * s)) for s in range(2)]
            out += [(t, 2, LAT, PAST, None)]
        else:
            lo, hi = max(tt - 1, 0), min(tt + 1, LAT // P - 1)
            out += [(t, 0, lo * P, (hi - lo + 1) * P, (lo - tt + 1) * P), (t, 1, LAT, PAST, None)]
    return out


def key_steps(kind, c):
    if c == 2:
        return [(LAT + PAST + P * k, 0, SEQ, None) for k in range(2)]
    out = [(LAT + P * k, 0, 512, None) for k in range(PAST // P)]
    for kt in range(LAT // P):
        if kind == "B":
            out.append((kt * P, 0, 512, None))
            continue
        if kind == "A":
            ts = [t for t in range(4) if key_tile0(4 * c + t) <= kt < key_tile0(4 * c + t) + 5]
        else:
            ts = [t for t in range(4) if abs(4 * c + t - kt) <= 1]
        if ts:
            q0, n = ts[0] * P, len(ts) * P
            tab = (kt - 2 * c) * 512 + q0 if kind == "A" else (4 * c + ts[0] - kt + 1) * P
            out.append((kt * P, q0, n, tab))
    return out


JOBS = attention_jobs()
NJ = len(JOBS)


def n_pieces(j):
    return len(row_pieces(JOBS[j][0], JOBS[j][3]))


def n_steps(j):
    return len(key_steps(JOBS[j][0], JOBS[j][3]))


def attention_slots():
    slots = [("first", 0, list(range(n_pieces(0))))]
    for j in range(NJ):
        s = n_steps(j)
        todo = list(range(n_pieces(j + 1))) if j + 1 < NJ else []
        rate = -(-len(todo) // max(1, s - 3)) if todo else 0
        for i in range(s):
            now, todo = todo[:rate], todo[rate:]
            last = bool(now) and not todo
            slots.append(("step", j, i, now, last))
        assert not todo
        slots.append(("end", j))
    return slots


SLOTS = attention_slots()
PIECES = sum(n_pieces(j) for j in range(NJ))
STEPS = sum(n_steps(j) for j in range(NJ))
PIECE0 = [sum(n_pieces(i) for i in range(j)) for j in range(NJ + 1)]
STEP0 = [sum(n_steps(i) for i in range(j)) for j in range(NJ + 1)]


def in_groups():
    gs = []
    for i, (kind, rows) in enumerate((("A", 0), ("A", 128), ("B", 0), ("B", 128), ("D", 0))):
        gs.append(dict(form="cache", kind=kind, row=rows, unit=-1, col=LAT, n=PAST, dst=("k", kind, rows)))
    for u, (form, kind, what) in enumerate(IN_UNITS):
        if form in "ts":
            for c, (c0, n) in enumerate(CHUNKS):
                for m in range(2 if form == "t" else 1):
                    rope = kind in "BD" and c < 2
                    col = c0 if what == "q" or c < 2 else LAT + PAST
                    gs.append(dict(form="rope" if rope else "t", unit=u, m=m, c=c, n=n, col=col, kind=kind,
                                   scale=QS if (what == "q" and kind != "B") else 1.0, dst=(what, kind, m * P)))
        if form in "ns" or (form == "t" and what == "k"):
            for t in range(TOK // P):
                if form == "t" and t < LAT // P:
                    continue
                gs.append(dict(form="n", unit=u, t=t, n=UW, nform=form))
    return gs


GROUPS = in_groups()
for _u in range(NU_IN):
    [g for g in GROUPS if g["unit"] == _u][-1]["last_of_unit"] = True
    [g for g in GROUPS if g["unit"] == _u][0]["first_of_unit"] = True
    [g for g in GROUPS if g["unit"] == _u][3]["fourth_of_unit"] = True
_t = _r = _n = 0
for _i, _g in enumerate(GROUPS):
    _g["i"] = _i
    if _g["form"] == "n":
        _g["ni"] = _n
        _n += 1
    else:
        _g["ti"] = _t
        _t += 1
    if _g["form"] == "rope":
        _g["ri"] = _r
        _r += 1
NG, NT, NR, NN = len(GROUPS), _t, _r, _n
_h = 0
for _i, _g in enumerate(GROUPS):
    for _x in ([_g] if _g["form"] in ("t", "cache") else []) + ([GROUPS[_i - 1]] if _i and GROUPS[_i - 1]["form"] == "rope" else []):
        _x["hi"] = _h
        _h += 1
assert _h == NT and GROUPS[-1]["form"] != "rope"


def n_stores(g):
    n = 1 if g["nform"] != "t" else 0
    if g["t"] >= LAT // P:
        n += 2 if g["nform"] == "s" else (g["unit"] in (1, 2, 4, 5))
    return n


_b = [0, 0]
for _g in GROUPS:
    if _g["form"] == "n":
        _g["stored_before"] = _b[_g["ni"] % 2]
        _b[_g["ni"] % 2] += 16 * n_stores(_g)
N_BYTES = _b
NDFT = 2 * (LAT // P) + SEQ // P
NR_DFT = 3
DFT_USES = [len(range(s, NDFT, NR_DFT)) for s in range(NR_DFT)]


def bias_parts(which):
    out = []
    if which == 0:
        for pi, t in enumerate((0, 1, 2, 6, 7)):
            for a in range(2):
                r = 2 * t + a
                w = row_window(r)
                out.append((a, pi * 640 + (w - 2 * key_tile0(t)) * 64, w - r + NA_KH - 1, NA_KH))
        return out
    r0 = 8 * (which - 1)
    for k in range(6):
        for b in range(2):
            rk = 2 * (2 * (which - 1) + k) + b
            rs = [r for r in range(r0, r0 + 8) if row_window(r) <= rk < row_window(r) + NA_KH]
            if rs:
                out.append((b, k * 512 + (rs[0] - r0) * 64, NA_KH - 1 - rk + rs[0], len(rs)))
    return out


STRIPS = [[(8, 49, 0, 1, NA_KW), (0, 8, 0, 0, NA_KW), (57, 7, 48, 0, NA_KW)],
          [(7, 49, 0, 1, NA_KW), (0, 7, 1, 1, 8), (56, 8, 49, 1, 8), (0, 16, 0, 0, 8), (48, 16, 56, 0, 8)]]


def check_strips():
    col = np.arange(GRID_W)
    cstart = np.clip(col - NA_KW // 2, 0, GRID_W - NA_KW)
    cmask = (col[None, :] >= cstart[:, None]) & (col[None, :] < cstart[:, None] + NA_KW)
    for mask, strips in ((cmask, STRIPS[0]), (cmask.T, STRIPS[1])):
        got = np.zeros_like(mask)
        for o, n, i, st, w in strips:
            for x in range(n):
                got[o + x, i + st * x:i + st * x + w] = True
        assert (got == mask).all()


check_strips()
BIAS_PARTS = [bias_parts(w) for w in range(3)]
ADDS = [(j, i) for j in range(NJ) for i, s in enumerate(key_steps(JOBS[j][0], JOBS[j][3])) if s[3] is not None]
ADD_INDEX = {ji: n for n, ji in enumerate(ADDS)}
NADD = len(ADDS)
ADD0 = [sum(1 for a in ADDS if a[0] < j) for j in range(NJ + 1)]
HEAD_DMAS = [{"B": 7, "A": 6, "D": 6}[JOBS[v * NCH][0]] + (3 if JOBS[v * NCH][2] == 0 else 0) for v in range(16)]
HEAD_IN = [16 * sum(HEAD_DMAS[u] for u in range(v + 1) if u % 2 == v % 2) for v in range(16)]
HEAD_ALL = [HEAD_IN[14], HEAD_IN[15]]


FIRST_D = [j[0] for j in JOBS].index("D")
NV = NJ // NCH
PAIRS = [v for v in range(NV) if JOBS[v * NCH][0] != "B" and JOBS[v * NCH][1] % 2 == 1]
NAO = (len(PAIRS) + 2) * NCH
RECIP_AT, SCALE_AT, PAIR_AT = (0, 5), (1, 1), [(1, 3), (1, 5), (1, 7)]
T_USES = [sum(1 for i in range(NT) if i % 2 == b) for b in range(2)]
N_USES = [sum(1 for i in range(NN) if i % 2 == b) for b in range(2)]
R_USES = [sum(1 for i in range(NR) if i % 2 == b) for b in range(2)]
Q_LAYER = NU_OUT * NCH * 2 + NB * NCH * KT
M_LAYER = NB * NCH * 2
NORMS = 2 * DEPTH + 1
FT = KT * NCH
PHASES = 2


def trunk(nc, I, O):
    ctx = ExitStack()

    ctx.enter_context(nc.allow_non_contiguous_dma(reason="small vectors are laid over the partitions"))

    def sem(name):
        return ctx.enter_context(nc.semaphore(name))

    base = -(-nc.sbuf_base // 64) * 64
    top = nc.sbuf_usable_end
    X0 = base
    H0 = X0 + KT * TOK * 4
    W0 = H0 + 2 * KT * TOK * 4
    C0 = W0 + 3 * 16384 + 8192
    cur = {"c": C0}

    def at(name, shape, dt, off):
        size = 4 * int(np.prod(shape[1:]))
        assert off + size <= top, (name, off + size, top)
        return nc.alloc_sbuf_tensor_at(name, shape, dt, offset=off).ap(), off + size

    def put(name, shape, dt=F32):
        ap, cur["c"] = at(name, shape, dt, cur["c"])
        cur["c"] = -(-cur["c"] // 32) * 32
        return ap

    xT, _ = at("xT", [P, KT, TOK], F32, X0)
    h_hi, _ = at("h_hi", [P, KT, TOK], F32R, H0)
    h_lo, _ = at("h_lo", [P, KT, TOK], F32R, H0 + KT * TOK * 4)
    w_hi, w_lo = [], []
    for s in range(3):
        a, o = at(f"w_hi{s}", [P, 2048], F32R, W0 + s * 16384)
        b, _ = at(f"w_lo{s}", [P, 2048], F32R, o)
        w_hi.append(a)
        w_lo.append(b)
    stage, _ = at("stage", [P, 2048], F32, W0 + 3 * 16384)
    ident = put("ident", [P, P])
    ones = put("ones_sq", [P, P])
    headsum = put("headsum", [P, P])
    swap = put("swap", [P, 2, P])
    pair = put("pair", [3, 2])
    mods = put("mods", [P, 48, 2])
    gains = put("gains", [P, 3, KT])
    mod_a = put("mod_a", [P, 2, KT, 2])
    fin_a = put("fin_a", [P, KT, 2])
    zero8 = put("zero8", [P, 8])
    eps_c = put("eps_c", [P, 1])
    cond = put("cond", [P, KT, 2])
    cond_t = put("cond_t", [P, 3, KT, 2])
    lam_v = put("lam_v", [P, 4, 32])
    lam_s = put("lam_s", [P, 8])
    lam_i = put("lam_i", [P, 1])
    sub_g = put("sub_g", [P, 2])
    sink_c = put("sink_c", [P, 4])
    TMP = cur["c"]

    def tmp(start=None):
        cur["c"] = TMP if start is None else start

    tmp()
    sq = [put(f"sq{i}", [P, 512]) for i in range(2)]
    xr = [put(f"xr{i}", [P, 512]) for i in range(2)]
    hf = [put(f"hf{i}", [P, 512]) for i in range(2)]
    std = put("std", [P, 512])
    rstd = [put(f"rstd{i}", [P, 512]) for i in range(2)]
    TMP2 = cur["c"]
    zf = [put(f"zf{i}", [P, 512]) for i in range(2)]
    z_hi = [put(f"z_hi{i}", [P, 512], F32R) for i in range(2)]
    z_lo = [put(f"z_lo{i}", [P, 512], F32R) for i in range(2)]
    vn = [put(f"vn{i}", [P, UW]) for i in range(2)]
    cache_n = put("cache_n", [P, 4, P])
    tmp()
    rope_t = [put(f"rope_t{i}", [P, 2, 512]) for i in range(2)]
    rp1 = put("rp1", [P, 512])
    rp2 = [put(f"rp2{i}", [P, 512]) for i in range(2)]
    zr = [put("zr0", [P, 512])]
    assert cur["c"] <= TMP2
    tmp(TMP2)
    m_hi = [put(f"m_hi{i}", [P, 2, 512], F32R) for i in range(2)]
    m_lo = [put(f"m_lo{i}", [P, 2, 512], F32R) for i in range(2)]
    m_r = [put(f"m_r{i}", [P, 512]) for i in range(2)]
    m_f = [put(f"m_f{i}", [P, 512]) for i in range(2)]
    ada_w = []
    off = H0
    for s in range(4):
        a, off = at(f"ada_w{s}", [P, KT, 512], F32, off)
        ada_w.append(a)
    m_row, _ = at("m_row", [3, 4, 512], F32, off)
    x_nat, _ = at("x_nat", [P, TOK // P, D], F32, W0)
    off = W0
    fc_n, off = at("fc_n", [P, TOK // P, 256], F32, off)
    dft_t = []
    for s in range(NR_DFT):
        a, off = at(f"dft_t{s}", [P, 2, 512], F32, off)
        dft_t.append(a)
    w_f, off = at("w_f", [P, 2, 256], F32, off)
    dft_ch, off = at("dft_ch", [P, 2, P], F32, off)
    g_cs, off = at("g_cs", [P, 2, 2, 256], F32, off)
    assert off <= W0 + 2 * 16384
    off = H0
    q1, q2, k1, k2, vv = [], [], [], [], []
    for s in range(2):
        for lst, nm, shp, dt in ((q1, "q1", [P, TOK], F32R), (q2, "q2", [96, TOK], F32R), (k1, "k1", [P, KEYS], F32R),
                                 (k2, "k2", [96, KEYS], F32R), (vv, "vv", [P, KEYS // P, P], F32)):
            a, off = at(f"{nm}_{s}", shp, dt, off)
            lst.append(a)
    NP_RING = 8
    prob = []
    for s in range(NP_RING):
        a, off = at(f"prob{s}", [P, 512], F32, off)
        prob.append(a)
    assert off <= W0
    off = W0
    na_q, off = at("na_q", [P, 5 * 640], F32, off)
    na_k = []
    for c in range(2):
        a, off = at(f"na_k{c}", [P, 6 * 512], F32, off)
        na_k.append(a)
    o_b, off = at("o_b", [P, 2, TOK], F32, off)
    o_ad, off = at("o_ad", [P, TOK], F32, off)
    sb = []
    for s in range(2):
        a, off = at(f"sb{s}", [P, 512], F32, off)
        sb.append(a)
    assert off <= C0
    cur["c"] = TMP
    swa_q, swa_k = put("swa_q", [P, 384]), put("swa_k", [P, 384])
    sink_rows = put("sink_rows", [P, 2, P])
    mp = put("mp", [P, 4, 4])
    mcol = [put(f"mcol{i}", [P, 4]) for i in range(2)]
    junk = put("junk", [P, 2, 384])
    f_ab, _ = at("f_ab", [P, 4, 512], F32, cur["c"])
    o_raw = [put(f"o_raw{i}", [P, TOK]) for i in range(2)]
    rden = put("rden", [P, TOK])
    den_c, den_r = put("den_c", [P, TOK // P]), put("den_r", [P, TOK // P])
    p_sink = put("p_sink", [P, 512])
    ao_hi = [put(f"ao_hi{i}", [P, 512], F32R) for i in range(NCH)]
    ao_lo = [put(f"ao_lo{i}", [P, 512], F32R) for i in range(NCH)]
    y_nat, _ = at("y_nat", [P, TOK // P, D], F32, W0)

    bank = ctx.enter_context(nc.psum_tensor("bank", [P, 8, 512], F32))

    def scratch(name, shape):
        return nc.dram_tensor(name, shape, F32).ap()

    s_q = {k: scratch(f"s_q{k}", [2, 256, TOK]) for k in "ABD"}
    s_k = {k: scratch(f"s_k{k}", [2, 256 if k != "D" else P, KEYS]) for k in "ABD"}
    s_v = scratch("s_v", [TOK, 1024])
    s_o = scratch("s_o", [2, D, TOK])
    s_den, s_rden = scratch("s_den", [16, TOK]), scratch("s_rden", [16, TOK])
    s_mods = scratch("s_mods", [DEPTH, P, 96])
    s_ones = scratch("s_ones", [1, KEYS])
    s_toe = scratch("s_toe", [DEPTH, 4, 2, GRID_W, BR * GRID_W])

    toe_neg, toe_in = sem("toe_neg"), sem("toe_in")
    phase, ones_in = sem("phase"), sem("ones_in")
    ada_ok, seen = sem("ada_ok"), sem("seen")
    const_in = sem("const_in")
    xin = sem("xin")
    cond_rdy, cond_e, cond_d = sem("cond_rdy"), sem("cond_e"), sem("cond_d")
    ada_in = [sem(f"ada_in{i}") for i in range(4)]
    ada_rows, ada_copied, ada_used, ada_modp, ada_mods, ada_saved = (sem("ada_rows"), sem("ada_copied"), sem("ada_used"),
                                                          sem("ada_modp"), sem("ada_mods"), sem("ada_saved"))
    xt_full, xt_free = sem("xt_full"), sem("xt_free")
    small_in, small_rdy, mod_rdy = sem("small_in"), sem("small_rdy"), sem("mod_rdy")
    stage_full, whi_rdy, wlo_rdy, w_used = sem("stage_full"), sem("whi_rdy"), sem("wlo_rdy"), sem("w_used")
    n_sq, n_squ, n_std, n_rs, n_t, n_f, n_hi, n_lo = (sem("n_sq"), sem("n_squ"), sem("n_std"), sem("n_rs"), sem("n_t"),
                                                      sem("n_f"), sem("n_hi"), sem("n_lo"))
    z_full = sem("z_full")
    zf_rdy, rp_full, rp_1, rp_2, zr_rdy, zhi_rdy, zlo_rdy = (sem("zf_rdy"), sem("rp_full"), sem("rp_1"), sem("rp_2"),
                                                             sem("zr_rdy"), sem("zhi_rdy"), sem("zlo_rdy"))
    z_out = [sem(f"z_out{i}") for i in range(2)]
    vn_rdy = sem("vn_rdy")
    vn_out = [sem(f"vn_out{i}") for i in range(2)]
    rope_in = [sem(f"rope_in{i}") for i in range(2)]
    cache_in = sem("cache_in")
    f_in = sem("f_in")
    dft_in = [sem(f"dft_in{i}") for i in range(NR_DFT)]
    dft_used, f_gp, f_g, f_full, f_ev, f_o, f_hi, f_lo = (sem("dft_used"), sem("f_gp"), sem("f_g"), sem("f_full"), sem("f_ev"),
                                                    sem("f_o"), sem("f_hi"), sem("f_lo"))
    a_init, a_tab = sem("a_init"), sem("a_tab")
    head_in = [sem(f"head_in{i}") for i in range(2)]
    b_in = [sem(f"b_in{i}") for i in range(3)]
    b_init = sem("b_init")
    s1_full, s1_max, m_col, m_rowp, m_rdy = sem("s1_full"), sem("s1_max"), sem("m_col"), sem("m_rowp"), sem("m_rdy")
    s2_full, s2_add, p_rdy, pv_done = sem("s2_full"), sem("s2_add"), sem("p_rdy"), sem("pv_done")
    sink_p, o_mul, o_free = sem("sink_p"), sem("o_mul"), sem("o_free")
    den_out, den_in, den_rdy, rden_out, rden_in = (sem("den_out"), sem("den_in"), sem("den_rdy"), sem("rden_out"),
                                                   sem("rden_in"))
    ao_h, ao_l, o_diff = sem("ao_h"), sem("ao_l"), sem("o_diff")
    ao_out = [sem(f"ao_out{i}") for i in range(NCH)]
    sn_sq, sn_full, sn_std, sn_r, sn_o = sem("sn_sq"), sem("sn_full"), sem("sn_std"), sem("sn_r"), sem("sn_o")
    lam_d, lam_e = sem("lam_d"), sem("lam_e")
    o_in = [sem(f"o_in{i}") for i in range(NCH)]
    q_full, q_free = sem("q_full"), sem("q_free")
    p1_full, r_rdy, sqr_rdy, mhi_rdy, mlo_rdy = (sem("p1_full"), sem("r_rdy"), sem("sqr_rdy"), sem("mhi_rdy"),
                                                 sem("mlo_rdy"))
    y_full, y_ev, y_out = sem("y_full"), sem("y_ev"), sem("y_out")

    def pair_index(v, c):
        return (PAIRS.index(v) if v < NV - 1 else NAO // NCH - 1) * NCH + c

    def settle(e):
        e.sem_inc(seen, 1)

    def barrier(e, k):
        settle(e)
        e.drain().then_inc(phase, 1)
        e.wait_ge(phase, 5 * k)
        settle(e)

    SLOT_OUT = [2, 0, 1, 2]

    def unit_slot(n):
        if n < NU_IN:
            return n % 3
        if n < NU_IN + NU_OUT:
            return SLOT_OUT[n - NU_IN]
        b, down = divmod(n - NU_IN - NU_OUT, 2)
        return 2 if down else b % 2

    def unit_prev(n):
        if n < NU_IN:
            return n - 3 if n >= 3 else None
        if n < NU_IN + NU_OUT:
            return NU_IN if n == NU_IN + 3 else None
        return n - 2 if (n - NU_IN - NU_OUT) % 2 else n - 4

    def hi_unit(pool, l, n, slot, prev):
        pool.wait_ge(stage_full, (l * U_LAYER + n + 1) * 16)
        if prev is not None:
            pool.wait_ge(w_used, l * U_LAYER + prev + 1 + 1)
        settle(pool)
        pool.tensor_scalar(w_hi[slot], stage, 1.0, 0.0, ALU.mult, ALU.add).then_inc(whi_rdy, 1)

    def lo_unit(dve, l, n, slot):
        dve.wait_ge(whi_rdy, l * U_LAYER + n + 1)
        dve.tensor_tensor(w_lo[slot], stage, w_hi[slot].bitcast(F32), ALU.subtract).then_inc(wlo_rdy, 1)

    def load_unit(sp, l, n, src):
        sp.wait_ge(wlo_rdy, l * U_LAYER + n + 1)
        sp.dma_start(stage.rearrange("p (k n) -> p k n", k=src.shape[1]), src).then_inc(stage_full, 16)

    w_in_v = I["w_in"].rearrange("l (k p) n -> l p k n", p=P)
    w_out_v = I["w_out"].rearrange("l (k p) n -> l p k n", p=P)
    w1_v = I["w_mlp1"].rearrange("l (k p) n -> l p k n", p=P)
    w2_v = I["w_mlp2"].rearrange("l (k p) n -> l p k n", p=P)
    w_ada_v = I["w_ada"].rearrange("l (k p) n -> l p k n", p=P)

    def norm_act(act, nn, x_at, final=None):
        def squares(c):
            c0, n = CHUNKS[c]
            x_at(act, c)
            for k in range(KT):
                i = (nn * NCH + c) * KT + k
                act.wait_ge(n_squ, i + 1)
                act.activation(sq[k % 2][:, :n], xT[:, k, c0:c0 + n], ACT.Square).then_inc(n_sq, 1)
            act.wait_ge(n_squ, (nn * NCH + c + 1) * KT + CREDIT)
            act.wait_ge(n_rs, nn * NCH + c + 1 + 1)
            act.activation(std[:, :n], bank[:, 6 + c % 2, :n], ACT.Sqrt, bias=eps_c, scale=1.0 / D).then_inc(n_std, 1)

        def upper(c):
            c0, n = CHUNKS[c]
            for k in range(KT):
                i = (nn * NCH + c) * KT + k
                act.wait_ge(n_f, i + 1 + CREDIT)
                act.activation(h_hi[:, k, c0:c0 + n], hf[k % 2][:, :n], ACT.Copy).then_inc(n_hi, 1)

        squares(0)
        for c in range(NCH):
            if c + 1 < NCH:
                squares(c + 1)
            if final:
                final(c)
            else:
                upper(c)

    def norm_pe(pe, nn, c):
        n = CHUNKS[c][1]
        for k in range(KT):
            i = (nn * NCH + c) * KT + k
            if k == 0:
                pe.wait_ge(n_std, nn * NCH + c + 1)
            pe.wait_ge(n_sq, i + 1)
            pe.matmul(bank[:, 6 + c % 2, :n], ones, sq[k % 2][:, :n], start=(k == 0),
                      stop=(k == KT - 1)).then_inc(n_squ, 1)

    def norm_dve(dve, nn, final=False):
        for c in range(NCH):
            c0, n = CHUNKS[c]
            q = nn * NCH + c
            dve.wait_ge(n_std, q + 1 + CREDIT)
            if c >= 2:
                dve.wait_ge(n_t, (q - 1) * KT)
            dve.reciprocal(rstd[c % 2][:, :n], std[:, :n]).then_inc(n_rs, 1)
            dve.wait_ge(n_rs, q + 1 + CREDIT)

            def lower(k):
                dve.wait_ge(n_hi, q * KT + k + 1 + CREDIT)
                dve.tensor_tensor(h_lo[:, k, c0:c0 + n], hf[k % 2][:, :n], h_hi[:, k, c0:c0 + n].bitcast(F32),
                                  ALU.subtract).then_inc(n_lo, 1)
            for k in range(KT):
                i = q * KT + k
                dve.wait_ge(n_f, i + 1)
                dve.tensor_tensor(xr[k % 2][:, :n], xT[:, k, c0:c0 + n], rstd[c % 2][:, :n], ALU.mult).then_inc(n_t, 1)
                if k and not final:
                    lower(k - 1)
            if not final:
                lower(KT - 1)

    def norm_pool(pool, nn, scale, shift, final=False):
        for c in range(NCH):
            n = CHUNKS[c][1]
            cd = 1 if c == 2 else 0
            for k in range(KT):
                i = (nn * NCH + c) * KT + k
                pool.wait_ge(n_t, i + 1)
                if final:
                    pool.wait_ge(y_full, (c * KT + k) + 1)
                else:
                    pool.wait_ge(n_hi, i + 1)
                    pool.wait_ge(n_lo, i + 1)
                settle(pool)
                pool.tensor_scalar(hf[k % 2][:, :n], xr[k % 2][:, :n], scale(k, cd), shift(k, cd), ALU.mult,
                                   ALU.add).then_inc(n_f, 1)

    def ones_row(n):
        return s_ones[0:1, 0:n]

    def y_ev_at(t):
        return (min(t // 4, 2) + 1) * KT

    block = ctx.enter_context(nc.Block())

    @block.sync
    def _(sp):
        sp.sem_inc(ada_ok, 1)
        for dst, src in ((ident, I["k_ident"]), (ones, I["k_ones"][:, 0:P]), (headsum, I["k_headsum"]),
                         (swap, I["k_swap"].rearrange("s p n -> p s n")), (pair, I["k_pair"]),
                         (fin_a[:, :, 0], I["final_g"].rearrange("(k p) -> p k", p=P))):
            sp.dma_start(dst, src).then_inc(const_in, 16)
        sp.dma_start(cond[:, :, 0], I["c"].rearrange("b (k p) -> p (b k)", p=P)).then_inc(const_in, 16)
        sp.dma_start(cond[:, :, 1], I["c_ctx"].rearrange("(k p) -> p k", p=P)).then_inc(const_in, 16)
        for t in range(TOK // P):
            src = I["x_sample"][0, t * P:(t + 1) * P] if t < LAT // P else I["x_prompt"][0, t * P - LAT:(t + 1) * P - LAT]
            sp.dma_start(x_nat[:, t], src).then_inc(xin, 16)
        with sp.Fori(0, DEPTH) as l:
            for n in range(12):
                s = n % 4
                sp.wait_ge(ada_used, l * 12 + n + 1)
                sp.dma_start(ada_w[s], w_ada_v[l, :, :, n * 512:(n + 1) * 512]).then_inc(ada_in[s], 16)
                sp.dma_start(m_row[2:3, s], I["b_ada"][l, n * 512:(n + 1) * 512].rearrange("(a n) -> a n", a=1)
                             ).then_inc(ada_in[s], 16)
            sp.wait_ge(ada_mods, l + 1 + 1)
            sp.dma_start(s_mods[l], mods.rearrange("p a b -> p (a b)")).then_inc(ada_saved, 16)
            sp.wait_ge(ada_saved, l * 16 + 16)
            sp.sem_inc(ada_ok, 1)
        sp.dma_start(s_ones, I["k_ones"][0:1, :]).then_inc(ones_in, 16)
        sp.wait_ge(ones_in, 16)
        barrier(sp, 1)

        with sp.Fori(0, DEPTH) as l:
            sp.dma_start(mods.rearrange("p a b -> p (a b)"), s_mods[l]).then_inc(small_in, 16)
            sp.dma_start(gains[:, 0], I["norm1_g"][l].rearrange("(k p) -> p k", p=P)).then_inc(small_in, 16)
            sp.dma_start(gains[:, 1], I["norm2_g"][l].rearrange("(k p) -> p k", p=P)).then_inc(small_in, 16)
            sp.dma_start(lam_i, bass.AP(tensor=I["k_lam_init"].tensor, offset=l, ap=[[0, P], [1, 1]])
                         ).then_inc(small_in, 16)
            for i, nm in enumerate(("diff_lq1", "diff_lk1", "diff_lq2", "diff_lk2")):
                sp.dma_start(lam_v[:, i], bass.AP(tensor=I[nm].tensor, offset=l * 32, ap=[[0, P], [1, 32]])
                             ).then_inc(small_in, 16)
            sp.dma_start(sink_c, bass.AP(tensor=I["swa_sink"].tensor, offset=l * 4, ap=[[0, P], [1, 4]])
                         ).then_inc(small_in, 16)
            for hh in range(2):
                sp.dma_start(sub_g[hh * 64:hh * 64 + 64, 0:1], I["diff_subln_g"][l].rearrange("(d a) -> d a", a=1)
                             ).then_inc(a_tab, 16)

            load_unit(sp, l, 0, w_in_v[l, :, :, 0:UW])
            load_unit(sp, l, 1, w_in_v[l, :, :, UW:2 * UW])

            cache_src = {"A": I["cache_na_k"], "B": I["cache_diff_k"], "D": I["cache_swa_k"]}

            def store(g):
                if g["form"] != "n":
                    s = g["hi"] % 2
                    sp.wait_ge(zlo_rdy, l * NT + g["hi"] + 1)
                    what, kind, row = g["dst"]
                    dst = (s_q if what == "q" else s_k)[kind]
                    for part, src in ((0, z_hi[s]), (1, z_lo[s])):
                        sp.dma_start(dst[part, row:row + P, g["col"]:g["col"] + g["n"]],
                                     src[:, :g["n"]].bitcast(F32)).then_inc(z_out[s], 16)
                    return
                s = g["ni"] % 2
                sp.wait_ge(vn_rdy, l * NN + g["ni"] + 1)
                t, form = g["t"], g["nform"]
                if form != "t":
                    c0 = 768 if form == "s" else IN_UNITS[g["unit"]][2]
                    sp.dma_start(s_v[t * P:(t + 1) * P, c0:c0 + UW], vn[s]).then_inc(vn_out[s], 16)
                name = {1: "o_na_k", 2: "o_na_v", 4: "o_df_k", 5: "o_df_v"}.get(g["unit"])
                if t >= LAT // P:
                    r0 = t * P - LAT
                    if name:
                        sp.dma_start(O[name][0, l, r0:r0 + P].rearrange("t h d -> t (h d)"), vn[s]).then_inc(vn_out[s], 16)
                    if form == "s":
                        sp.dma_start(O["o_sw_k"][0, l, r0:r0 + P].rearrange("t h d -> t (h d)"), vn[s][:, 0:P]
                                     ).then_inc(vn_out[s], 16)
                        sp.dma_start(O["o_sw_v"][0, l, r0:r0 + P].rearrange("t h d -> t (h d)"), vn[s][:, P:UW]
                                     ).then_inc(vn_out[s], 16)

            for g in GROUPS:
                if g["form"] == "cache":
                    if g["i"]:
                        sp.wait_ge(z_full, l * NG + g["i"])
                    sp.dma_start(cache_n, cache_src[g["kind"]][0, l].rearrange("(t p) h d -> p t (h d)", p=P)[
                        :, :, g["row"]:g["row"] + P]).then_inc(cache_in, 16)
                if g.get("first_of_unit") and g["unit"] + 2 < NU_IN:
                    u = g["unit"] + 2
                    load_unit(sp, l, u, w_in_v[l, :, :, u * UW:(u + 1) * UW])
                if g["form"] == "rope":
                    r = g["ri"]
                    if r == 0:
                        sp.wait_ge(n_lo, l * (2 * NCH * KT) + (NCH * KT + CREDIT))
                    sp.wait_ge(rp_1, l * NR + r + 1)
                    sp.wait_ge(rp_2, l * NR + r + 1)
                    kd = 0 if g["kind"] == "B" else 1
                    sp.dma_start(rope_t[r % 2], I["k_rope"][kd, :, :, g["c"] * 512:(g["c"] + 1) * 512].rearrange(
                        "s p n -> p s n")).then_inc(rope_in[r % 2], 16)
                if g["i"] >= 1:
                    store(GROUPS[g["i"] - 1])
            store(GROUPS[-1])
            for s in range(2):
                sp.wait_ge(z_out[s], (l + 1) * T_USES[s] * 32)
                settle(sp)
                sp.wait_ge(vn_out[s], (l + 1) * N_BYTES[s])
            barrier(sp, l * PHASES + 2)

            def load_dft(i):
                c, kt = (i // 8, i % 8) if i < 16 else (2, i - 16)
                c0, n = CHUNKS[c]
                tab, cc = (I["k_dft_lat"], c0) if c < 2 else (I["k_dft_ctx"], 0)
                if i >= NR_DFT:
                    sp.wait_ge(dft_used, l * NDFT + i - NR_DFT + 1)
                sp.dma_start(dft_t[i % NR_DFT][:, :, :n], tab[:, kt * P:(kt + 1) * P, cc:cc + n].rearrange(
                    "s p n -> p s n")).then_inc(dft_in[i % NR_DFT], 16)

            def load_fourier():
                sp.dma_start(fc_n, s_v[:, 512:768].rearrange("(t p) n -> p t n", p=P)).then_inc(f_in, 16)
                sp.dma_start(w_f, I["w_fourier"][l].rearrange("(k p) n -> p k n", p=P)).then_inc(f_in, 16)
                sp.dma_start(dft_ch, I["k_dft_ch"].rearrange("s p n -> p s n")).then_inc(f_in, 16)
                for i in range(NR_DFT):
                    load_dft(i)


            def load_head(v):
                kind, h, half, _, _ = JOBS[v * NCH]
                b, vb = v % 2, h % 2
                if v >= 2:
                    sp.wait_ge(pv_done, l * STEPS + STEP0[(v - 1) * NCH])
                S = head_in[b]
                if kind == "B":
                    r0 = h * 64 + half * 32
                    parts_q = [(0, 0), (32, 1), (64, 0)]
                    parts_k = [(0, 0), (32, 0), (64, 1)]
                    for (row, part), (rk, pk) in zip(parts_q, parts_k):
                        sp.dma_start(q1[b][row:row + 32].bitcast(F32), s_q["B"][part, r0:r0 + 32]).then_inc(S, 16)
                        sp.dma_start(k1[b][rk:rk + 32].bitcast(F32), s_k["B"][pk, r0:r0 + 32]).then_inc(S, 16)
                    sp.dma_start(k1[b][96:97].bitcast(F32), ones_row(KEYS)).then_inc(S, 16)
                else:
                    r0 = h * 64
                    rk = h * 64 if kind == "A" else (h // 2) * 64
                    for part in range(2):
                        sp.dma_start(q1[b][part * 64:part * 64 + 64].bitcast(F32), s_q[kind][part, r0:r0 + 64]
                                     ).then_inc(S, 16)
                        sp.dma_start(k1[b][part * 64:part * 64 + 64].bitcast(F32), s_k[kind][0, rk:rk + 64]
                                     ).then_inc(S, 16)
                    sp.dma_start(q2[b][0:64].bitcast(F32), s_q[kind][0, r0:r0 + 64]).then_inc(S, 16)
                    sp.dma_start(k2[b][0:64].bitcast(F32), s_k[kind][1, rk:rk + 64]).then_inc(S, 16)
                if half == 0:
                    c0 = {"A": h * 64, "B": 256 + h * 64, "D": 896 + (h // 2) * 64}[kind]
                    cache = {"A": I["cache_na_v"], "B": I["cache_diff_v"], "D": I["cache_swa_v"]}[kind]
                    hk = h // 2 if kind == "D" else h
                    vs = slice(vb * 64, vb * 64 + 64)
                    sp.dma_start(vv[vb][:, 0:8, vs], s_v[0:LAT, c0:c0 + 64].rearrange("(t p) d -> p t d", p=P)
                                 ).then_inc(S, 16)
                    sp.dma_start(vv[vb][:, 8:12, vs], cache[0, l, :, hk].rearrange("(t p) d -> p t d", p=P)
                                 ).then_inc(S, 16)
                    sp.dma_start(vv[vb][:, 12:14, vs], s_v[LAT:TOK, c0:c0 + 64].rearrange("(t p) d -> p t d", p=P)
                                 ).then_inc(S, 16)

            def load_bias(h, which):
                dst = (na_q, na_k[0], na_k[1])[which]
                for half, c0, r, n in BIAS_PARTS[which]:
                    sp.dma_start(dst[half * 64:half * 64 + 64, c0:c0 + n * 64],
                                 s_toe[l, h, min(which, 1), :, r * 64:(r + n) * 64]).then_inc(b_in[which], 16)

            stored = [0]

            def denominators(v):
                h = JOBS[v * NCH][1]
                d = 64 - 64 * (h % 2)
                sp.wait_ge(o_free, l * NJ + (v + 1) * NCH)
                sp.dma_start(s_den[v:v + 1], o_raw[v % 2][d:d + 1]).then_inc(den_out, 16)
                sp.wait_ge(den_out, l * NV * 16 + (v + 1) * 16)
                sp.dma_start(den_c, s_den[v].rearrange("(p t) -> p t", p=P)).then_inc(den_in, 16)

            def reciprocals(v):
                h = JOBS[v * NCH][1]
                o = 64 * (h % 2)
                sp.wait_ge(den_rdy, l * NV + v + 1)
                sp.dma_start(s_rden[v].rearrange("(p t) -> p t", p=P), den_r).then_inc(rden_out, 16)
                sp.wait_ge(rden_out, l * NV * 16 + (v + 1) * 16)
                if v:
                    sp.wait_ge(o_mul, l * NV + v)
                sp.dma_start(rden[o:o + 64], bass.AP(tensor=s_rden.tensor, offset=v * TOK, ap=[[0, 64], [1, TOK]])
                             ).then_inc(rden_in, 16)

            def store_out(kind, h2, c):
                i = stored[0]
                s = i % NCH
                c0, n = CHUNKS[c]
                r0 = {"A": 0, "B": 256, "D": 768}[kind] + h2 * P
                sp.wait_ge(ao_l, l * NAO + i + 1)
                for part, src in ((0, ao_hi[s]), (1, ao_lo[s])):
                    sp.dma_start(s_o[part, r0:r0 + P, c0:c0 + n], src[:, :n].bitcast(F32)).then_inc(ao_out[s], 16)
                stored[0] += 1

            load_head(0)
            sp.dma_start(swa_q, I["k_swa_mask_q"]).then_inc(a_tab, 16)
            sp.dma_start(swa_k, I["k_swa_mask_k"]).then_inc(a_tab, 16)
            sp.dma_start(sink_rows, I["k_sink_rows"].rearrange("s p n -> p s n")).then_inc(a_tab, 16)
            for j, (kind, h, half, c, v) in enumerate(JOBS):
                if j == FIRST_D + 1:
                    sp.wait_ge(s1_max, l * PIECES + PIECE0[FIRST_D])
                    settle(sp)
                    sp.wait_ge(s2_add, l * NADD + ADD0[FIRST_D])
                    settle(sp)
                    load_fourier()
                if c == 0:
                    if v + 1 < NV:
                        load_head(v + 1)
                    if v:
                        denominators(v - 1)
                        reciprocals(v - 1)
                    if v == 1:
                        sp.wait_ge(b_init, l * 3 + 3)
                        settle(sp)
                        for w in range(3):
                            load_bias(0, w)
                if kind == "A" and h < 3:
                    if c == 1:
                        sp.wait_ge(s1_max, l * PIECES + PIECE0[j + 1])
                        load_bias(h + 1, 0)
                        sp.wait_ge(s2_add, l * NADD + ADD0[j])
                        load_bias(h + 1, 1)
                    if c == 2:
                        sp.wait_ge(s2_add, l * NADD + ADD0[j])
                        load_bias(h + 1, 2)
                if c == 1 and v - 1 in PAIRS:
                    for cc in range(NCH):
                        store_out(JOBS[j - NCH][0], JOBS[j - NCH][1] // 2, cc)
            denominators(NV - 1)
            dft = iter(range(NR_DFT, NDFT))
            load_dft(next(dft))
            store_out("B", 0, 0)
            reciprocals(NV - 1)
            for x in range(1, 2 * NCH):
                load_dft(next(dft))
                store_out("B", x % 2, x // 2)
            for cc in range(NCH):
                load_dft(next(dft))
                store_out(JOBS[NJ - 1][0], JOBS[NJ - 1][1] // 2, cc)

            load_unit(sp, l, NU_IN, w_out_v[l, :, :, 0:UW])
            for s in range(NCH):
                sp.wait_ge(ao_out[s], (l + 1) * (NAO // NCH) * 32)
                settle(sp)
            sp.wait_ge(pv_done, (l + 1) * STEPS)
            settle(sp)
            for c, (c0, n) in enumerate(CHUNKS):
                for part, dst in ((0, h_hi), (1, h_lo)):
                    for k0, k1_ in ((0, 4), (6, 8)):
                        sp.dma_start(dst[:, k0:k1_, c0:c0 + n].bitcast(F32), s_o[part, k0 * P:k1_ * P, c0:c0 + n].rearrange(
                            "(k p) n -> p k n", p=P)).then_inc(o_in[c], 16)
                    for i in (next(dft, None),) + ((next(dft, None),) if c == 0 else ()):
                        if i is not None:
                            load_dft(i)
            assert next(dft, None) is None
            n0 = NU_IN
            for u in range(1, NU_OUT):
                load_unit(sp, l, n0 + u, w_out_v[l, :, :, u * UW:(u + 1) * UW])

            def load_up(b):
                load_unit(sp, l, NU_IN + NU_OUT + 2 * b, w1_v[l, :, :, bass.ds(b * UW, UW)])

            def load_down(b):
                load_unit(sp, l, NU_IN + NU_OUT + 2 * b + 1, w2_v[l, :, bass.ds(b * 2, 2), :])

            load_up(0)
            load_down(0)
            with sp.Fori(0, NB // 2 - 1) as i:
                for bb in range(2):
                    load_up(i * 2 + bb + 1)
                    load_down(i * 2 + bb + 1)
            load_up(NB - 1)
            load_down(NB - 1)
            barrier(sp, l * PHASES + 3)

        for t in range(TOK // P):
            sp.wait_ge(y_ev, y_ev_at(t))
            dst = O["y_sample"][0, t * P:(t + 1) * P] if t < LAT // P else O["y_prompt"][0, t * P - LAT:(t + 1) * P - LAT]
            sp.dma_start(dst, y_nat[:, t]).then_inc(y_out, 16)
        sp.wait_ge(y_out, (TOK // P) * 16)

    SMALL0, SMALL = 0, 9

    @block.gpsimd
    def _(pool):
        pool.sem_inc(n_f, CREDIT)
        pool.sem_inc(mhi_rdy, CREDIT)
        pool.sem_inc(rp_2, CREDIT)
        barrier(pool, 1)
        with pool.Fori(0, DEPTH) as l:
            hi_unit(pool, l, 0, 0, None)
            hi_unit(pool, l, 1, 1, None)
            pool.wait_ge(mod_rdy, l * 4 + 4)
            norm_pool(pool, l * 2, lambda k, cd: mod_a[:, 0, k, cd:cd + 1], lambda k, cd: mods[:, k, cd:cd + 1])

            def turned(g):
                r = g["ri"]
                pool.wait_ge(zf_rdy, l * NR + r + 1)
                pool.wait_ge(rope_in[r % 2], l * R_USES[r % 2] * 16 + (r // 2 + 1) * 16)
                pool.wait_ge(zr_rdy, l * NR + r + 1)
                pool.tensor_tensor(rp2[r % 2], zf[r % 2], rope_t[r % 2][:, 0], ALU.mult).then_inc(rp_2, 1)

            for g in GROUPS:
                if g["i"] and GROUPS[g["i"] - 1]["form"] == "rope":
                    turned(GROUPS[g["i"] - 1])
                if g.get("first_of_unit") and g["unit"] + 2 < NU_IN:
                    u = g["unit"] + 2
                    hi_unit(pool, l, u, unit_slot(u), unit_prev(u))
            barrier(pool, l * PHASES + 2)
            for tab in (na_q, na_k[0], na_k[1]):
                pool.memset(tab, NEG).then_inc(b_init, 1)
            pool.wait_ge(sn_o, l * 6 + 6)
            pool.wait_ge(ao_l, (l + 1) * NAO)
            for u in range(NU_OUT):
                if u == 1:
                    pool.wait_ge(f_o, (l + 1) * NCH * 2)
                n = NU_IN + u
                hi_unit(pool, l, n, unit_slot(n), unit_prev(n))
            n = NU_IN + NU_OUT
            hi_unit(pool, l, n, unit_slot(n), NU_IN + 1)
            pool.wait_ge(q_full, l * Q_LAYER + NU_OUT * NCH * 2)
            hi_unit(pool, l, n + 1, unit_slot(n + 1), None)
            norm_pool(pool, l * 2 + 1, lambda k, cd: mod_a[:, 1, k, cd:cd + 1], lambda k, cd: mods[:, 24 + k, cd:cd + 1])

            def block_(b, bb, last):
                for c in range(NCH):
                    n_ = CHUNKS[c][1]
                    for m in range(2):
                        x = b * 6 + (c * 2 + m)
                        buf = (bb * 3 + c) % 2
                        pool.wait_ge(sqr_rdy, l * M_LAYER + x + 1 + CREDIT)
                        pool.wait_ge(q_full, l * Q_LAYER + b * (NCH * KT) + (NU_OUT * NCH * 2 + (c - 1) * KT))
                        settle(pool)
                        pool.tensor_scalar(m_hi[buf][:, m, :n_], m_f[m][:, :n_], 1.0, 0.0, ALU.mult, ALU.add
                                           ).then_inc(mhi_rdy, 1)
                    if c == 0 and not last:
                        u = NU_IN + NU_OUT + b * 2 + 2
                        hi_unit(pool, l, u, (bb + 1) % 2, u - 4)
                if not last:
                    u = NU_IN + NU_OUT + b * 2 + 3
                    hi_unit(pool, l, u, 2, u - 2)

            with pool.Fori(0, NB // 2 - 1) as i:
                for bb in range(2):
                    block_(i * 2 + bb, bb, False)
            for bb in range(2):
                block_(NB - 2 + bb, bb, bb == 1)
            barrier(pool, l * PHASES + 3)
        norm_pool(pool, 2 * DEPTH, lambda k, cd: fin_a[:, k, 0:1], lambda k, cd: zero8[:, 0:1], final=True)

    @block.scalar
    def _(act):
        act.sem_inc(ada_copied, CREDIT)
        act.sem_inc(n_std, CREDIT)
        act.sem_inc(n_hi, CREDIT)
        act.sem_inc(r_rdy, 4)
        for l in range(DEPTH):
            for h in range(0, 4):
                act.dma_start(s_toe[l, h].rearrange("r c x -> (r c) x"), I["k_neg"]).then_inc(toe_neg, 16)
        act.wait_ge(const_in, 8 * 16)
        act.activation(cond_t[:, 0], cond, ACT.Exp, scale=-1.0).then_inc(cond_e, 1)
        def expand(l, h, r, strip):
            row = BR * GRID_W
            o, n, i, st, w = strip
            src = bass.AP(tensor=(I["na_rpb"] if r == 0 else I["na_rpb_rev"]).tensor,
                          offset=(l * 4 + h) * BR * BC + (i - o) + NA_KW - 1, ap=[[BC, BR], [st - 1, n], [1, w]])
            dst = bass.AP(tensor=s_toe.tensor, offset=((l * 4 + h) * 2 + r) * GRID_W * row + o * row + i,
                          ap=[[GRID_W, BR], [row + st, n], [1, w]])
            act.dma_start(dst, src).then_inc(toe_in, 16)

        tables = [(l, h, r) for l in range(DEPTH) for h in range(4) for r in range(2)]
        first = [(*t, x) for t in tables for x in STRIPS[t[2]][:3]]
        second = [(*t, x) for t in tables for x in STRIPS[t[2]][3:]]
        for q in range(DEPTH * 12):
            act.wait_ge(ada_rows, q + 1)
            act.wait_ge(ada_used, q + 1)
            act.activation(m_row[0:2, q % 4], bank[0:2, q % 2, :], ACT.Copy).then_inc(ada_copied, 1)
            if q == 0:
                act.wait_ge(toe_neg, DEPTH * 4 * 16)
            for x in first[4 * q:4 * q + 4]:
                expand(*x)
            if q == 14:
                act.wait_ge(toe_in, len(first) * 16)
            for x in second[4 * (q - 14):4 * (q - 14) + 4] if q >= 14 else []:
                expand(*x)
        act.wait_ge(toe_in, (len(first) + len(second)) * 16)
        barrier(act, 1)
        with act.Fori(0, DEPTH) as l:
            def upper(g, src):
                s = g["hi"] % 2
                if g["hi"] >= 2:
                    act.wait_ge(z_out[s], l * T_USES[s] * 32 + (g["hi"] // 2) * 32)
                act.activation(z_hi[s][:, :g["n"]], src[:, :g["n"]], ACT.Copy, scale=g.get("scale", 1.0)
                               if g["form"] != "rope" else 1.0).then_inc(zhi_rdy, 1)

            def evacuate(g):
                act.wait_ge(z_full, l * NG + g["i"] + 1)
                src = bank[:, g["i"] % 4]
                if g["form"] in ("t", "cache"):
                    upper(g, src)
                elif g["form"] == "rope":
                    r = g["ri"]
                    act.wait_ge(rp_full, l * NR + r + 1)
                    act.wait_ge(rp_2, l * NR + r + 1)
                    act.activation(zf[r % 2], src, ACT.Copy, scale=g["scale"]).then_inc(zf_rdy, 1)
                else:
                    s = g["ni"] % 2
                    if g["ni"] >= 2:
                        act.wait_ge(vn_out[s], l * N_BYTES[s] + g["stored_before"])
                    act.activation(vn[s], src[:, :UW], ACT.Copy).then_inc(vn_rdy, 1)
                if g["i"] and GROUPS[g["i"] - 1]["form"] == "rope":
                    p = GROUPS[g["i"] - 1]
                    act.wait_ge(zr_rdy, l * NR + p["ri"] + 1 + CREDIT)
                    upper(p, zr[0])

            for g in GROUPS[:5]:
                evacuate(g)
            norm_act(act, l * 2, lambda e, c: None)
            for g in GROUPS[5:]:
                evacuate(g)
            barrier(act, l * PHASES + 2)

            act.wait_ge(lam_d, l * 5 + 2)
            act.activation(lam_s[:, 2:4], lam_s[:, 0:2], ACT.Exp).then_inc(lam_e, 1)
            act.wait_ge(a_init, l + 1)

            def max_row(j):
                kind, _, _, c, v = JOBS[j]
                c0, n = CHUNKS[c]
                r, dst = (96, q1[v % 2]) if kind == "B" else (64, q2[v % 2])
                act.wait_ge(m_rowp, l * NJ + j + 1)
                act.activation(dst[r:r + 1, c0:c0 + n], bank[r:r + 1, 7, :n], ACT.Copy, scale=-1.0).then_inc(m_rdy, 1)

            def exponentials(j, i):
                kind = JOBS[j][0]
                _, _, n, tab = key_steps(kind, JOBS[j][3])[i]
                si = STEP0[j] + i
                if si >= NP_RING:
                    act.wait_ge(pv_done, l * STEPS + si - NP_RING + 1)
                if tab is None:
                    act.wait_ge(s2_full, l * STEPS + si + 1)
                    src = bank[:, 3 + si % 2, :n]
                else:
                    a = ADD_INDEX[(j, i)]
                    act.wait_ge(s2_add, l * NADD + a + 1)
                    src = sb[a % 2][:, :n]
                act.activation(prob[si % NP_RING][:, :n], src, ACT.Exp, scale=FS if kind == "B" else 1.0
                               ).then_inc(p_rdy, 1)

            def sink_row(j):
                _, h, _, c, v = JOBS[j]
                c0, n = CHUNKS[c]
                act.wait_ge(pv_done, l * STEPS + STEP0[j])
                act.wait_ge(m_rdy, l * NJ + j + 1)
                act.activation(p_sink[64:65, :n], q2[v % 2][64:65, c0:c0 + n].bitcast(F32), ACT.Exp,
                               bias=sink_c[64:65, h:h + 1]).then_inc(sink_p, 1)

            def upper_out(idx, src, n):
                s = idx % NCH
                if idx >= NCH:
                    act.wait_ge(ao_out[s], l * (NAO // NCH) * 32 + (idx // NCH) * 32)
                act.activation(ao_hi[s][:, :n], src, ACT.Copy).then_inc(ao_h, 1)

            def upper_pair(v, c):
                c0, n = CHUNKS[c]
                act.wait_ge(o_mul, l * NV + v + 1)
                upper_out(pair_index(v, c), o_ad[:, c0:c0 + n], n)

            def take(j):
                c0, n = CHUNKS[JOBS[j][3]]
                v = JOBS[j][4]
                act.wait_ge(pv_done, l * STEPS + STEP0[j + 1])
                if v >= 2:
                    act.wait_ge(o_mul, l * NV + v - 1)
                act.activation(o_raw[v % 2][:, c0:c0 + n], bank[:, 5 + j % 2, :n], ACT.Copy).then_inc(o_free, 1)

            due = False
            for slot in SLOTS:
                if slot[0] == "first":
                    max_row(0)
                elif slot[0] == "step":
                    _, j, i, _, last = slot
                    exponentials(j, i)
                    if due:
                        max_row(j + 1)
                    due = last
                    if i == 0 and JOBS[j][0] == "D":
                        sink_row(j)
                    if i == 1 and j:
                        take(j - 1)
                    if JOBS[j][4] - 1 in PAIRS and (JOBS[j][3], i) in PAIR_AT:
                        upper_pair(JOBS[j][4] - 1, PAIR_AT.index((JOBS[j][3], i)))
            take(NJ - 1)
            for x in range(2 * NCH):
                c, h2 = divmod(x, 2)
                c0, n = CHUNKS[c]
                act.wait_ge(pv_done, (l + 1) * STEPS)
                act.activation(prob[x][:, :n], o_b[:, h2, c0:c0 + n], ACT.Square).then_inc(sn_sq, 1)
            for x in range(2 * NCH):
                n = CHUNKS[x // 2][1]
                act.wait_ge(sn_full, l * 6 + x + 1)
                act.activation(prob[x][:, :n], bank[:, x % 2, :n], ACT.Sqrt, bias=eps_c, scale=1.0 / HD).then_inc(sn_std, 1)
            for x in range(2 * NCH):
                n = CHUNKS[x // 2][1]
                act.wait_ge(sn_o, l * 6 + x + 1)
                upper_out(NAO - NCH * 3 + x, prob[x][:, :n], n)
            for c in range(NCH):
                upper_pair(NV - 1, c)

            for c, (c0, n) in enumerate(CHUNKS):
                for m in range(2):
                    act.wait_ge(f_o, (l * NCH + c) * 2 + m + 1)
                    act.activation(h_hi[:, 4 + m, c0:c0 + n], bank[:, 6 + m, :n], ACT.Copy).then_inc(f_hi, 1)

            def x_at(e, c):
                e.wait_ge(q_free, l * Q_LAYER + (NU_OUT - 1) * NCH * 2 + c * 2 + 2 + CREDIT)
            norm_act(act, l * 2 + 1, x_at)

            def block_(b, bb):
                for c in range(NCH):
                    n = CHUNKS[c][1]
                    for m in range(2):
                        x = b * 6 + (c * 2 + m)
                        act.wait_ge(p1_full, l * M_LAYER + x + 1)
                        act.wait_ge(sqr_rdy, l * M_LAYER + x + 1)
                        act.activation(m_r[m][:, :n], bank[:, (bb * 6 + c * 2 + m) % 4, :n], ACT.Relu).then_inc(r_rdy, 1)

            with act.Fori(0, NB // 2 - 1) as i:
                for bb in range(2):
                    block_(i * 2 + bb, bb)
            for bb in range(2):
                block_(NB - 2 + bb, bb)
            barrier(act, l * PHASES + 3)

        def rows(c):
            n = CHUNKS[c][1]
            for k in range(KT):
                i = c * KT + k
                act.wait_ge(y_full, i + 1 + CREDIT)
                act.activation(y_nat[:, 4 * c:4 * c + n // P, k * P:(k + 1) * P],
                               bank[:, i % 4, :n].rearrange("p (t f) -> p t f", f=P), ACT.Copy).then_inc(y_ev, 1)
        norm_act(act, 2 * DEPTH, lambda e, c: None, final=rows)

    @block.vector
    def _(dve):
        dve.sem_inc(n_rs, CREDIT)
        dve.sem_inc(n_lo, CREDIT)
        dve.sem_inc(wlo_rdy, 1)
        dve.sem_inc(ada_mods, 1)
        dve.sem_inc(rp_1, CREDIT)
        dve.sem_inc(zr_rdy, CREDIT)
        dve.sem_inc(q_free, CREDIT)
        dve.sem_inc(sqr_rdy, CREDIT)
        dve.sem_inc(mlo_rdy, CREDIT)
        dve.memset(eps_c, EPS)
        dve.memset(zero8, 0.0)
        dve.wait_ge(cond_e, 1)
        dve.tensor_scalar(cond_t[:, 1], cond_t[:, 0], 1.0, None, ALU.add).then_inc(cond_d, 1)
        dve.wait_ge(cond_d, 1)
        dve.reciprocal(cond_t[:, 2], cond_t[:, 1]).then_inc(cond_d, 1)
        dve.wait_ge(cond_d, 2)
        dve.tensor_tensor(cond, cond, cond_t[:, 2], ALU.mult).then_inc(cond_d, 1)
        for i in range(FT):
            c, k = divmod(i, KT)
            c0, n = CHUNKS[c]
            dve.wait_ge(xt_full, i + 1)
            dve.tensor_copy(xT[:, k, c0:c0 + n], bank[:, 4 + i % 4, :n]).then_inc(xt_free, 1)
        with dve.Fori(0, DEPTH) as l:
            dve.wait_ge(ada_modp, l + 1)
            dve.wait_ge(ada_ok, l + 1)
            dve.tensor_copy(mods.rearrange("p a b -> p (a b)"), bank[:, 3, 0:96]).then_inc(ada_mods, 1)
        barrier(dve, 1)

        with dve.Fori(0, DEPTH) as l:
            dve.wait_ge(small_in, l * SMALL * 16 + (SMALL0 + SMALL) * 16)
            for w in range(2):
                for cd in range(2):
                    g0 = 8 * (3 * w + 1)
                    dve.scalar_tensor_tensor(out=mod_a[:, w, :, cd], in0=mods[:, g0:g0 + KT, cd], scalar=1.0,
                                             in1=gains[:, w], op0=ALU.add, op1=ALU.mult).then_inc(mod_rdy, 1)
            dve.tensor_tensor_reduce(rp1[:, 0:32], lam_v[:, 0], lam_v[:, 1], 1.0, 0.0, ALU.mult, ALU.add,
                                     lam_s[:, 0:1]).then_inc(lam_d, 1)
            dve.tensor_tensor_reduce(rp1[:, 32:64], lam_v[:, 2], lam_v[:, 3], 1.0, 0.0, ALU.mult, ALU.add,
                                     lam_s[:, 1:2]).then_inc(lam_d, 1)

            def lower(g, src, scale):
                s = g["hi"] % 2
                n = g["n"]
                dve.wait_ge(zhi_rdy, l * NT + g["hi"] + 1)
                dve.scalar_tensor_tensor(out=z_lo[s][:, :n], in0=src[:, :n], scalar=scale, in1=z_hi[s][:, :n].bitcast(F32),
                                         op0=ALU.mult, op1=ALU.subtract).then_inc(zlo_rdy, 1)

            def evacuate(g):
                if g["form"] in ("t", "cache"):
                    lower(g, bank[:, g["i"] % 4], g.get("scale", 1.0))
                if g["i"] and GROUPS[g["i"] - 1]["form"] == "rope":
                    p = GROUPS[g["i"] - 1]
                    r = p["ri"]
                    dve.wait_ge(rp_full, l * NR + r + 1 + CREDIT)
                    dve.wait_ge(rope_in[r % 2], l * R_USES[r % 2] * 16 + (r // 2 + 1) * 16)
                    dve.tensor_tensor(rp1, bank[:, 4 + r % 2], rope_t[r % 2][:, 1], ALU.mult).then_inc(rp_1, 1)
                    dve.wait_ge(rp_1, l * NR + r + 1 + CREDIT)
                    dve.wait_ge(rp_2, l * NR + r + 1 + CREDIT)
                    dve.tensor_tensor(zr[0], rp1, rp2[r % 2], ALU.add).then_inc(zr_rdy, 1)
                    lower(p, zr[0], 1.0)
                if g.get("fourth_of_unit") and g["unit"] + 2 < NU_IN:
                    lo_unit(dve, l, g["unit"] + 2, unit_slot(g["unit"] + 2))

            lo_unit(dve, l, 0, 0)
            lo_unit(dve, l, 1, 1)
            for g in GROUPS[:5]:
                evacuate(g)
            norm_dve(dve, l * 2)
            for g in GROUPS[5:]:
                evacuate(g)
            barrier(dve, l * PHASES + 2)

            for b in range(2):
                dve.memset(q2[b][64:96].bitcast(F32), 0.0)
                dve.memset(k2[b][64:96].bitcast(F32), 1.0)
                dve.memset(vv[b][:, :, 64 * (1 - b):64 * (1 - b) + 64], 1.0)
            dve.memset(p_sink, 0.0).then_inc(a_init, 1)
            dve.wait_ge(lam_e, l + 1)
            dve.wait_ge(a_tab, l * 80 + 80)
            dve.tensor_tensor(lam_s[:, 4:5], lam_s[:, 3:4], lam_s[:, 2:3], ALU.subtract).then_inc(lam_d, 1)
            dve.tensor_scalar(lam_s[:, 6:7], lam_i, -1.0, 1.0, ALU.mult, ALU.add).then_inc(lam_d, 1)
            dve.wait_ge(lam_d, l * 5 + 4)
            dve.tensor_tensor(lam_s[:, 5:6], lam_s[:, 4:5], lam_i, ALU.subtract)
            dve.tensor_tensor(sub_g[:, 1:2], sub_g[:, 0:1], lam_s[:, 6:7], ALU.mult).then_inc(lam_d, 1)
            dve.wait_ge(lam_d, l * 5 + 5)

            def table_ready(kind, h, which):
                if kind == "A":
                    n = 16 * len(BIAS_PARTS[which])
                    dve.wait_ge(b_in[which], l * 4 * n + (h + 1) * n)

            def piece(j, p):
                kind, h, _, c, v = JOBS[j]
                t, x, _, n, tab = row_pieces(kind, c)[p]
                gi = PIECE0[j] + p
                np_ = len({q[1] for q in row_pieces(kind, c)})
                if p == 0 and j:
                    dve.wait_ge(m_col, l * NJ + j)
                if kind == "D" and p == 0:
                    nt = CHUNKS[c][1] // P
                    dve.tensor_scalar(mp[:, 0:nt, np_], zero8[:, 0:nt], sink_c[:, h:h + 1], None, ALU.add)
                dve.wait_ge(s1_full, l * PIECES + gi + 1)
                src = bank[:, gi % 3, :n]
                if tab is None:
                    dve.tensor_reduce(mp[:, t, x:x + 1], src, AX.X, ALU.max).then_inc(s1_max, 1)
                else:
                    table_ready(kind, h, 0)
                    table = (na_q if kind == "A" else swa_q)[:, tab:tab + n]
                    if gi >= 2:
                        dve.wait_ge(s1_max, l * PIECES + gi - 1)
                    settle(dve)
                    dve.tensor_tensor_reduce(junk[:, gi % 2, :n], src, table, 1.0, 3.0 * NEG, ALU.add, ALU.max,
                                             mp[:, t, x:x + 1]).then_inc(s1_max, 1)

            def maxima(j):
                kind, _, _, c, _ = JOBS[j]
                nt = CHUNKS[c][1] // P
                np_ = len({q[1] for q in row_pieces(kind, c)}) + (kind == "D")
                dve.wait_ge(s1_max, l * PIECES + PIECE0[j + 1])
                if j >= 2:
                    dve.wait_ge(m_rowp, l * NJ + j - 1)
                dve.tensor_reduce(mcol[j % 2][:, 0:nt], mp[:, 0:nt, 0:np_], AX.X, ALU.max).then_inc(m_col, 1)

            def add_bias(j, i):
                kind, h, _, c, _ = JOBS[j]
                _, _, n, tab = key_steps(kind, c)[i]
                a, si = ADD_INDEX[(j, i)], STEP0[j] + i
                dve.wait_ge(s2_full, l * STEPS + si + 1)
                table_ready(kind, h, 1 + c)
                if a >= 2:
                    pj, pi = ADDS[a - 2]
                    dve.wait_ge(p_rdy, l * STEPS + STEP0[pj] + pi + 1)
                table = (na_k[c] if kind == "A" else swa_k)[:, tab:tab + n]
                dve.tensor_tensor(sb[a % 2][:, :n], bank[:, 3 + si % 2, :n], table, ALU.add).then_inc(s2_add, 1)

            def invert(v):
                dve.wait_ge(den_in, l * NV * 16 + (v + 1) * 16)
                if v:
                    dve.wait_ge(rden_out, l * NV * 16 + v * 16)
                dve.reciprocal(den_r, den_c).then_inc(den_rdy, 1)

            def scale(v):
                kind, h, half, _, _ = JOBS[v * NCH]
                o = slice(64 * (h % 2), 64 * (h % 2) + 64)
                raw = o_raw[v % 2][o]
                dve.wait_ge(rden_in, l * NV * 16 + (v + 1) * 16)
                if kind != "B":
                    done = sum(1 for p in PAIRS if p < v) * NCH
                    if done:
                        dve.wait_ge(ao_h, l * NAO + done)
                        dve.wait_ge(ao_l, l * NAO + done)
                    dve.tensor_tensor(o_ad[o], raw, rden[o], ALU.mult).then_inc(o_mul, 1)
                elif half == 0:
                    dve.tensor_tensor(o_b[o, h // 2], raw, rden[o], ALU.mult).then_inc(o_mul, 1)
                else:
                    dve.tensor_tensor(raw, raw, rden[o], ALU.mult).then_inc(o_diff, 1)
                    dve.wait_ge(o_diff, l * 4 + h + 1)
                    dve.scalar_tensor_tensor(out=o_b[o, h // 2], in0=raw, scalar=lam_s[o, 5:6], in1=o_b[o, h // 2],
                                             op0=ALU.mult, op1=ALU.add).then_inc(o_mul, 1)

            def lower_out(idx, src, n):
                dve.wait_ge(ao_h, l * NAO + idx + 1)
                dve.tensor_tensor(ao_lo[idx % NCH][:, :n], src, ao_hi[idx % NCH][:, :n].bitcast(F32), ALU.subtract
                                  ).then_inc(ao_l, 1)

            def lower_pair(v, c):
                c0, n = CHUNKS[c]
                lower_out(pair_index(v, c), o_ad[:, c0:c0 + n], n)

            for slot in SLOTS:
                if slot[0] == "first":
                    for p in slot[2]:
                        piece(0, p)
                    maxima(0)
                elif slot[0] == "step":
                    _, j, i, now, last = slot
                    if (j, i) in ADD_INDEX:
                        add_bias(j, i)
                    for p in now:
                        piece(j + 1, p)
                    if last:
                        maxima(j + 1)
                    v, at_ = JOBS[j][4], (JOBS[j][3], i)
                    if v and at_ == RECIP_AT:
                        invert(v - 1)
                    if v and at_ == SCALE_AT:
                        scale(v - 1)
                    if v - 1 in PAIRS and (at_[0], i - 1) in PAIR_AT:
                        lower_pair(v - 1, PAIR_AT.index((at_[0], i - 1)))
            for m in range(2):
                dve.wait_ge(f_gp, l + 1)
                dve.tensor_copy(g_cs[:, m], bank[:, m].rearrange("p (s n) -> p s n", s=2)).then_inc(f_g, 1)
            for x in range(2 * NCH):
                c, h2 = divmod(x, 2)
                c0, n = CHUNKS[c]
                dve.wait_ge(sn_std, l * 6 + x + 1)
                if x == 2:
                    invert(NV - 1)
                if x == 4:
                    scale(NV - 1)
                dve.reciprocal(sb[x % 2][:, :n], prob[x][:, :n]).then_inc(sn_r, 1)
                dve.wait_ge(sn_r, l * 6 + x + 1)
                dve.scalar_tensor_tensor(out=prob[x][:, :n], in0=o_b[:, h2, c0:c0 + n], scalar=sub_g[:, 1:2],
                                         in1=sb[x % 2][:, :n], op0=ALU.mult, op1=ALU.mult).then_inc(sn_o, 1)
                lower_out(NAO - NCH * 3 + x, prob[x][:, :n], n)
            for c in range(NCH):
                lower_pair(NV - 1, c)
            dve.wait_ge(ao_h, (l + 1) * NAO)
            for c, (c0, n) in enumerate(CHUNKS):
                dve.wait_ge(f_full, l * NCH + c + 1)
                if c:
                    dve.wait_ge(f_o, (l * NCH + c) * 2)
                for x in range(4):
                    dve.tensor_copy(f_ab[:, x, :n], bank[:, 2 + x, :n]).then_inc(f_ev, 1)
                if c == 1:
                    lo_unit(dve, l, NU_IN, unit_slot(NU_IN))
                for m in range(2):
                    dve.wait_ge(f_hi, (l * NCH + c) * 2 + m + 1)
                    dve.tensor_tensor(h_lo[:, 4 + m, c0:c0 + n], bank[:, 6 + m, :n], h_hi[:, 4 + m, c0:c0 + n].bitcast(F32),
                                      ALU.subtract).then_inc(f_lo, 1)

            def residual(l, gate, q, bk, k, c):
                c0, n = CHUNKS[c]
                cd = 1 if c == 2 else 0
                dve.wait_ge(q_full, q + 1)
                x = xT[:, k, c0:c0 + n]
                dve.scalar_tensor_tensor(out=x, in0=bank[:, bk, :n], scalar=mods[:, gate + k, cd:cd + 1], in1=x,
                                         op0=ALU.mult, op1=ALU.add).then_inc(q_free, 1)

            lo_unit(dve, l, NU_IN + 1, unit_slot(NU_IN + 1))
            for u in range(NU_OUT):
                for c in range(NCH):
                    for m in range(2):
                        q = (u * NCH + c) * 2 + m
                        residual(l, 16, l * Q_LAYER + q, 4 + q % 2, 2 * u + m, c)
                lo_unit(dve, l, NU_IN + u + 2, unit_slot(NU_IN + u + 2))
            norm_dve(dve, l * 2 + 1)

            def block_(b, bb, last):
                def hidden(c):
                    n = CHUNKS[c][1]
                    for m in range(2):
                        x = b * 6 + (c * 2 + m)
                        buf = (bb * 3 + c) % 2
                        dve.wait_ge(r_rdy, l * M_LAYER + x + 1 + 4)
                        dve.wait_ge(mhi_rdy, l * M_LAYER + x + 1)
                        dve.wait_ge(mlo_rdy, l * M_LAYER + x + 1)
                        dve.tensor_tensor(m_f[m][:, :n], m_r[m][:, :n], m_r[m][:, :n], ALU.mult).then_inc(sqr_rdy, 1)
                    for m in range(2):
                        x = b * 6 + (c * 2 + m)
                        dve.wait_ge(mhi_rdy, l * M_LAYER + x + 1 + CREDIT)
                        dve.tensor_tensor(m_lo[buf][:, m, :n], m_f[m][:, :n], m_hi[buf][:, m, :n].bitcast(F32),
                                          ALU.subtract).then_inc(mlo_rdy, 1)

                def down(c):
                    for k in range(KT):
                        q = b * (NCH * KT) + (NU_OUT * NCH * 2 + c * KT + k)
                        residual(l, 40, l * Q_LAYER + q, 4 + k % 2, k, c)

                hidden(0)
                if not last:
                    lo_unit(dve, l, NU_IN + NU_OUT + b * 2 + 2, (bb + 1) % 2)
                hidden(1)
                down(0)
                hidden(2)
                down(1)
                down(2)
                if not last:
                    lo_unit(dve, l, NU_IN + NU_OUT + b * 2 + 3, 2)

            with dve.Fori(0, NB // 2 - 1) as i:
                for bb in range(2):
                    block_(i * 2 + bb, bb, False)
            for bb in range(2):
                block_(NB - 2 + bb, bb, bb == 1)
            barrier(dve, l * PHASES + 3)
        norm_dve(dve, 2 * DEPTH, final=True)

    @block.tensor
    def _(pe):
        pe.sem_inc(ada_used, 4)
        pe.sem_inc(n_squ, CREDIT)
        pe.sem_inc(rp_full, CREDIT)
        pe.sem_inc(y_full, CREDIT)
        pe.wait_ge(const_in, 8 * 16)
        pe.wait_ge(xin, (TOK // P) * 16)
        for i in range(FT):
            c, k = divmod(i, KT)
            if i >= 4:
                pe.wait_ge(xt_free, i - 3)
            nt = CHUNKS[c][1] // P
            for t in range(nt):
                mm = pe.transpose(bank[:, 4 + i % 4, t * P:(t + 1) * P], x_nat[:, 4 * c + t, k * P:(k + 1) * P], ident)
            mm.then_inc(xt_full, 1)
        pe.wait_ge(cond_d, 3)
        with pe.Fori(0, DEPTH) as l:
            def columns(n):
                pe.wait_ge(ada_copied, l * 12 + n + 1 + CREDIT)
                if n == 0:
                    pe.wait_ge(ada_mods, l + 1)
                for j in range(4):
                    x = (n * 4 + j) * 2
                    mm = pe.matmul(bank[:, 3, x:x + 2], m_row[0:3, n % 4, j * P:(j + 1) * P], pair, start=True, stop=True)
                    if j == 3 and n < 11:
                        mm.then_inc(ada_used, 1)
                return mm
            for n in range(12):
                pe.wait_ge(ada_in[n % 4], l * 96 + (n // 4 + 1) * 32)
                pe.wait_ge(ada_copied, l * 12 + n + 1)
                for k in range(KT):
                    mm = pe.matmul(bank[0:2, n % 2, :], cond[:, k], ada_w[n % 4][:, k], start=(k == 0), stop=(k == KT - 1))
                mm.then_inc(ada_rows, 1)
                if n:
                    columns(n - 1)
            columns(11).then_inc(ada_modp, 1)
            pe.wait_ge(ada_modp, l + 1)
            pe.sem_inc(ada_used, 1)
        barrier(pe, 1)

        def three(out, a_hi, a_lo, b_hi, b_lo, first, last):
            x = pe.matmul(out, a_hi, b_hi, start=first, stop=False)
            pe.matmul(out, a_hi, b_lo, start=False, stop=False)
            return x, pe.matmul(out, a_lo, b_hi, start=False, stop=last)

        with pe.Fori(0, DEPTH) as l:
            def in_group(g):
                i = g["i"]
                if i >= 4:
                    p = GROUPS[i - 4]
                    if p["form"] == "rope":
                        pe.wait_ge(zf_rdy, l * NR + p["ri"] + 1)
                    elif p["form"] == "n":
                        pe.wait_ge(vn_rdy, l * NN + p["ni"] + 1)
                    else:
                        pe.wait_ge(zlo_rdy, l * NT + p["hi"] + 1)
                out = bank[:, i % 4, :g["n"]]
                if g["form"] == "cache":
                    pe.wait_ge(cache_in, l * 80 + (i + 1) * 16)
                    for t in range(4):
                        mm = pe.transpose(out[:, t * P:(t + 1) * P], cache_n[:, t], ident)
                    mm.then_inc(z_full, 1)
                    return
                u = g["unit"]
                if g.get("first_of_unit"):
                    pe.wait_ge(wlo_rdy, l * U_LAYER + u + 1 + 1)
                s = unit_slot(u)
                for k in range(KT):
                    if g["form"] == "n":
                        t = slice(g["t"] * P, (g["t"] + 1) * P)
                        w = slice(k * UW, (k + 1) * UW)
                        x, mm = three(out, h_hi[:, k, t], h_lo[:, k, t], w_hi[s][:, w], w_lo[s][:, w], k == 0, k == KT - 1)
                    else:
                        w = slice(k * UW + g["m"] * P, k * UW + (g["m"] + 1) * P)
                        c0, n = CHUNKS[g["c"]]
                        t = slice(c0, c0 + n)
                        x, mm = three(out, w_hi[s][:, w], w_lo[s][:, w], h_hi[:, k, t], h_lo[:, k, t], k == 0, k == KT - 1)
                    if k == 0 and g.get("first_of_unit"):
                        x.then_inc(w_used, 1)
                mm.then_inc(z_full, 1)

            def swapped(g):
                r = g["ri"]
                pe.wait_ge(zf_rdy, l * NR + r + 1)
                pe.wait_ge(rp_1, l * NR + r + 1)
                pe.matmul(bank[:, 4 + r % 2], swap[:, 0 if g["kind"] == "B" else 1], zf[r % 2], start=True, stop=True
                          ).then_inc(rp_full, 1)

            for g in GROUPS[:5]:
                in_group(g)
            norm_pe(pe, l * 2, 0)
            norm_pe(pe, l * 2, 1)
            for g in GROUPS[5:]:
                if g["unit"] == 0 and g["m"] == 0:
                    if g["c"] == 1:
                        norm_pe(pe, l * 2, 2)
                    pe.wait_ge(n_lo, (l * 2 * NCH + g["c"] + 1) * KT + CREDIT)
                in_group(g)
                if GROUPS[g["i"] - 1]["form"] == "rope":
                    swapped(GROUPS[g["i"] - 1])
            barrier(pe, l * PHASES + 2)

            pe.wait_ge(a_init, l + 1)
            pe.wait_ge(a_tab, l * 80 + 80)

            def piece(j, p):
                kind, _, _, c, v = JOBS[j]
                t, _, key0, n, _ = row_pieces(kind, c)[p]
                gi = PIECE0[j] + p
                if c == 0 and p == 0:
                    pe.wait_ge(head_in[v % 2], l * HEAD_ALL[v % 2] + HEAD_IN[v])
                if gi >= 3:
                    pe.wait_ge(s1_max, l * PIECES + gi - 2)
                q0 = CHUNKS[c][0] + t * P
                rows = 96 if kind == "B" else P
                pe.matmul(bank[:, gi % 3, :n], q1[v % 2][0:rows, q0:q0 + P], k1[v % 2][0:rows, key0:key0 + n],
                          start=True, stop=True).then_inc(s1_full, 1)

            def max_row(j):
                kind, _, _, c, _ = JOBS[j]
                r = 96 if kind == "B" else 64
                pe.wait_ge(m_col, l * NJ + j + 1)
                if j:
                    pe.wait_ge(m_rdy, l * NJ + j)
                for t in range(CHUNKS[c][1] // P):
                    mm = pe.matmul(bank[r:r + 1, 7, t * P:(t + 1) * P], mcol[j % 2][:, t:t + 1], ident, start=True, stop=True)
                mm.then_inc(m_rowp, 1)

            def scores(j, i):
                kind, _, _, c, v = JOBS[j]
                key0, q0, n, _ = key_steps(kind, c)[i]
                si = STEP0[j] + i
                if i == 0:
                    pe.wait_ge(m_rdy, l * NJ + j + 1)
                if si >= 2:
                    pe.wait_ge(p_rdy, l * STEPS + si - 1)
                q = slice(CHUNKS[c][0] + q0, CHUNKS[c][0] + q0 + n)
                k = slice(key0, key0 + P)
                out = bank[:, 3 + si % 2, :n]
                b = v % 2
                if kind == "B":
                    mm = pe.matmul(out, k1[b][0:97, k], q1[b][0:97, q], start=True, stop=True)
                else:
                    pe.matmul(out, k1[b][:, k], q1[b][:, q], start=True, stop=False)
                    mm = pe.matmul(out, k2[b][:, k], q2[b][:, q], start=False, stop=True)
                mm.then_inc(s2_full, 1)

            def values(j, i):
                kind, h, _, c, v = JOBS[j]
                steps = key_steps(kind, c)
                key0, q0, n, _ = steps[i]
                si = STEP0[j] + i
                ob = bank[:, 5 + j % 2]
                if i == 0 and j >= 2:
                    pe.wait_ge(o_free, l * NJ + j - 1)
                if i == 0 and kind == "D":
                    d = sum(1 for x in JOBS[:j] if x[0] == "D")
                    pe.wait_ge(sink_p, l * 4 * NCH + d + 1)
                    nn = CHUNKS[c][1]
                    pe.matmul(ob[:, :nn], sink_rows[:, h % 2], p_sink[:, :nn], start=True, stop=False)
                pe.wait_ge(p_rdy, l * STEPS + si + 1)
                pe.matmul(ob[:, q0:q0 + n], vv[h % 2][:, key0 // P], prob[si % NP_RING][:, :n],
                          start=(i == 0 and kind != "D"), stop=(i == len(steps) - 1)).then_inc(pv_done, 1)

            due = False
            for slot in SLOTS:
                if slot[0] == "first":
                    for p in slot[2]:
                        piece(0, p)
                    max_row(0)
                elif slot[0] == "step":
                    _, j, i, now, last = slot
                    scores(j, i)
                    for p in now:
                        piece(j + 1, p)
                    if due:
                        max_row(j + 1)
                    due = last
                    if i:
                        values(j, i - 1)
                else:
                    values(slot[1], n_steps(slot[1]) - 1)
            pe.wait_ge(s1_max, (l + 1) * PIECES)
            pe.wait_ge(f_in, (l + 1) * 48)
            for m in range(2):
                for s in range(2):
                    mm = pe.matmul(bank[:, m, s * 256:(s + 1) * 256], dft_ch[:, s], w_f[:, m], start=True, stop=True)
            mm.then_inc(f_gp, 1)
            for x in range(2 * NCH):
                n = CHUNKS[x // 2][1]
                pe.wait_ge(sn_sq, l * 6 + x + 1)
                pe.wait_ge(f_g, (l + 1) * 2)
                if x >= 2:
                    pe.wait_ge(sn_std, l * 6 + x - 1)
                pe.matmul(bank[:, x % 2, :n], headsum, prob[x][:, :n], start=True, stop=True).then_inc(sn_full, 1)
            pe.wait_ge(o_free, (l + 1) * NJ)
            i = 0
            for c, (c0, n) in enumerate(CHUNKS):
                if c:
                    pe.wait_ge(f_ev, (l * NCH + c) * 4)
                kts = LAT // P if c < 2 else SEQ // P
                for kt in range(kts):
                    s = i % NR_DFT
                    pe.wait_ge(dft_in[s], l * DFT_USES[s] * 16 + (i // NR_DFT + 1) * 16)
                    for m in range(2):
                        for cs in range(2):
                            mm = pe.matmul(bank[:, 2 + m * 2 + cs, :n], fc_n[:, kt + (8 if c == 2 else 0), m * P:(m + 1) * P],
                                           dft_t[s][:, cs, :n], start=(kt == 0), stop=(kt == kts - 1))
                    if kt < kts - 1:
                        mm.then_inc(dft_used, 1)
                    i += 1
                mm.then_inc(f_full, 1)
                pe.wait_ge(f_full, l * NCH + c + 1)
                pe.sem_inc(dft_used, 1)
                pe.wait_ge(f_ev, (l * NCH + c + 1) * 4)
                pe.wait_ge(f_g, (l + 1) * 2)
                if c:
                    pe.wait_ge(f_lo, (l * NCH + c) * 2)
                for m2 in range(2):
                    for x in range(4):
                        mm = pe.matmul(bank[:, 6 + m2, :n], g_cs[:, x // 2, x % 2, m2 * P:(m2 + 1) * P], f_ab[:, x, :n],
                                       start=(x == 0), stop=(x == 3))
                    mm.then_inc(f_o, 1)

            for u in range(NU_OUT):
                s = unit_slot(NU_IN + u)
                pe.wait_ge(wlo_rdy, l * U_LAYER + NU_IN + u + 1 + 1)
                for c, (c0, n) in enumerate(CHUNKS):
                    if u == 0:
                        pe.wait_ge(o_in[c], (l + 1) * 64)
                        pe.wait_ge(f_lo, (l * NCH + c + 1) * 2)
                    for m in range(2):
                        q = (u * NCH + c) * 2 + m
                        pe.wait_ge(q_free, l * Q_LAYER + q + 1)
                        for k in range(KT):
                            w = slice(k * UW + m * P, k * UW + (m + 1) * P)
                            x, mm = three(bank[:, 4 + q % 2, :n], w_hi[s][:, w], w_lo[s][:, w], h_hi[:, k, c0:c0 + n],
                                          h_lo[:, k, c0:c0 + n], k == 0, k == KT - 1)
                            if k == 0 and c == 0 and m == 0:
                                x.then_inc(w_used, 1)
                        mm.then_inc(q_full, 1)
            for c in range(NCH):
                norm_pe(pe, l * 2 + 1, c)

            def block_(b, bb):
                def up(c):
                    c0, n = CHUNKS[c]
                    s = bb
                    if c == 0:
                        pe.wait_ge(wlo_rdy, l * U_LAYER + b * 2 + (NU_IN + NU_OUT + 1 + 1))
                    pe.wait_ge(n_lo, l * (2 * NCH * KT) + ((NCH + c + 1) * KT + CREDIT))
                    for m in range(2):
                        bk = (bb * 6 + c * 2 + m) % 4
                        x_ = b * 6 + (c * 2 + m)
                        pe.wait_ge(r_rdy, l * M_LAYER + x_ + 1)
                        for k in range(KT):
                            w = slice(k * UW + m * P, k * UW + (m + 1) * P)
                            x, mm = three(bank[:, bk, :n], w_hi[s][:, w], w_lo[s][:, w], h_hi[:, k, c0:c0 + n],
                                          h_lo[:, k, c0:c0 + n], k == 0, k == KT - 1)
                            if k == 0 and c == 0 and m == 0:
                                x.then_inc(w_used, 1)
                        mm.then_inc(p1_full, 1)

                def down(c):
                    n = CHUNKS[c][1]
                    buf = (bb * 3 + c) % 2
                    if c == 0:
                        pe.wait_ge(wlo_rdy, l * U_LAYER + b * 2 + (NU_IN + NU_OUT + 2 + 1))
                    pe.wait_ge(mlo_rdy, l * M_LAYER + b * 6 + (c + 1) * 2 + CREDIT)
                    for k in range(KT):
                        q = b * (NCH * KT) + (NU_OUT * NCH * 2 + c * KT + k)
                        pe.wait_ge(q_free, l * Q_LAYER + q + 1)
                        for f in range(2):
                            w = slice(f * D + k * P, f * D + (k + 1) * P)
                            x, mm = three(bank[:, 4 + k % 2, :n], w_hi[2][:, w], w_lo[2][:, w], m_hi[buf][:, f, :n],
                                          m_lo[buf][:, f, :n], f == 0, f == 1)
                            if k == 0 and f == 0 and c == 1:
                                x.then_inc(w_used, 1)
                        mm.then_inc(q_full, 1)

                up(0)
                up(1)
                down(0)
                up(2)
                down(1)
                down(2)

            with pe.Fori(0, NB // 2) as i:
                for bb in range(2):
                    block_(i * 2 + bb, bb)
            barrier(pe, l * PHASES + 3)

        def rows(c):
            for k in range(KT):
                i = c * KT + k
                pe.wait_ge(n_f, (2 * DEPTH * NCH + c) * KT + k + 1 + CREDIT)
                if i >= 4:
                    pe.wait_ge(y_ev, i - 3)
                for t in range(CHUNKS[c][1] // P):
                    mm = pe.transpose(bank[:, i % 4, t * P:(t + 1) * P], hf[k % 2][:, t * P:(t + 1) * P], ident)
                mm.then_inc(y_full, 1)

        norm_pe(pe, 2 * DEPTH, 0)
        for c in range(NCH):
            if c + 1 < NCH:
                norm_pe(pe, 2 * DEPTH, c + 1)
            rows(c)


_INS = ["x_prompt", "x_sample", "cache_na_k", "cache_na_v", "cache_diff_k", "cache_diff_v", "cache_swa_k", "cache_swa_v",
        "c", "c_ctx", "w_ada", "b_ada", "norm1_g", "norm2_g", "w_in", "na_rpb", "diff_lq1", "diff_lk1", "diff_lq2",
        "diff_lk2", "diff_subln_g", "w_fourier", "swa_sink", "w_out", "w_mlp1", "w_mlp2", "final_g"]
_OUTS = [("y_prompt", (1, SEQ, D)), ("y_sample", (1, LAT, D)), ("o_na_k", (1, DEPTH, SEQ, 4, HD)),
         ("o_na_v", (1, DEPTH, SEQ, 4, HD)), ("o_df_k", (1, DEPTH, SEQ, 4, HD)), ("o_df_v", (1, DEPTH, SEQ, 4, HD)),
         ("o_sw_k", (1, DEPTH, SEQ, 2, HD)), ("o_sw_v", (1, DEPTH, SEQ, 2, HD))]


def kernel(**inputs):
    import concourse.bacc as bacc
    from concourse.bass_utils import run_bass_kernel_spmd as run

    nc = bacc.Bacc("TRN2", target_bir_lowering=False, num_devices=1, dynamic_dma_scratch_size=1024)
    arrays = {n: np.ascontiguousarray(inputs[n]) for n in _INS}
    arrays["na_rpb_rev"] = np.ascontiguousarray(arrays["na_rpb"][..., ::-1, ::-1])
    arrays.update({"k_" + n: a for n, a in CONST.items()})
    I = {n: nc.dram_tensor("in_" + n, a.shape, F32, kind="ExternalInput").ap() for n, a in arrays.items()}
    O = {n: nc.dram_tensor("out_" + n, shape, F32, kind="ExternalOutput").ap() for n, shape in _OUTS}
    trunk(nc, I, O)
    r = run(nc, [{"in_" + n: a for n, a in arrays.items()}], core_ids=[0])
    return tuple(r.results[0]["out_" + n] for n, _ in _OUTS)
```
